# Optimizing a Trainium2 kernel written in Bass

```python
import jax
import jax.numpy as jnp
from jax import lax
import numpy as np

'''One inference step of a hybrid decoder trunk (DEPTH layers) for a prompt group and a sample group sharing the same weights.

Per layer (pre-RMSNorm residual sub-layers):
  h = RMSNorm(x); [q|k|v|glu_a|glu_b] = h @ w_in   (one combined projection, columns split among head groups)
  group A: sliding-window GQA (window 128), QK-norm, ALiBi, learned per-head sinks, banded 128-query blocks
  group B: Conformer conv module: GLU -> causal depthwise conv (width 31) -> LayerNorm over channels -> swish
  x += concat(A, B) @ w_out   (w_out doubles as the conv module's final pointwise projection)
  x += CrossAttn(RMSNorm(x), memory K/V)   (4 heads, QK-norm, no positional term)
  x += HierMoE(RMSNorm(x))   (top-1 expert group, then top-2 SwiGLU experts inside it)

Inputs:
  x_prompt (BATCH, SEQ, D_MODEL), positions 0..SEQ-1
  x_sample (DEC_BATCH, DEC_SEQ, D_MODEL), positions PAST_LEN..PAST_LEN+DEC_SEQ-1
  cache_swa_k, cache_swa_v (DEPTH, DEC_BATCH, min(WINDOW, PAST_LEN), N_KV_HEADS, HEAD_DIM): normalised keys / values of
      positions PAST_LEN-min(WINDOW,PAST_LEN) .. PAST_LEN-1, oldest first
  state_conv (DEPTH, DEC_BATCH, CONV_WIDTH-1, D_CONV): last 30 GLU outputs (inputs of the depthwise conv)
  cache_mem_k, cache_mem_v (DEPTH, DEC_BATCH, MEM_LEN, MEM_HEADS, MEM_HEAD_DIM): memory keys (normalised) / values
  mem_prompt (BATCH, MEM_LEN, D_MODEL)
  weights, each with a leading DEPTH axis.
Returns the tuple
  (y_prompt (BATCH, SEQ, D_MODEL),
   y_sample (DEC_BATCH, DEC_SEQ, D_MODEL),
   swa_k_prompt, swa_v_prompt (DEPTH, BATCH, min(WINDOW, SEQ), N_KV_HEADS, HEAD_DIM),
   conv_prompt (DEPTH, BATCH, CONV_WIDTH-1, D_CONV),
   mem_k_prompt, mem_v_prompt (DEPTH, BATCH, MEM_LEN, MEM_HEADS, MEM_HEAD_DIM),
   swa_k_sample, swa_v_sample (DEPTH, DEC_BATCH, min(WINDOW, PAST_LEN), N_KV_HEADS, HEAD_DIM),
   conv_sample (DEPTH, DEC_BATCH, CONV_WIDTH-1, D_CONV))
'''

D_MODEL = 1024
BATCH = 1
SEQ = 1024
DEPTH = 1
DEC_BATCH = 8
DEC_SEQ = 8
PAST_LEN = 2048
PAGE_SIZE = 128

D_ATTN = D_MODEL // 2
D_CONV = D_MODEL - D_ATTN
HEAD_DIM = 64
N_HEADS = D_ATTN // HEAD_DIM
N_KV_HEADS = 2
KV_DIM = N_KV_HEADS * HEAD_DIM
WINDOW = 128
BLOCK = 128
CONV_WIDTH = 31
CONV_GROUPS = 8
MEM_LEN = 256
MEM_HEADS = 4
MEM_HEAD_DIM = D_MODEL // MEM_HEADS
N_GROUPS = 4
EXPERTS_PER_GROUP = 8
N_EXPERTS = N_GROUPS * EXPERTS_PER_GROUP
TOP_K = 2
D_EXPERT = D_MODEL // 4
D_IN = D_ATTN + 2 * KV_DIM + 2 * D_CONV
EPS = 1e-6
NEG_INF = -1e30

kernel_name = 'hymba_swa_conformer_hmoe_step'

def rmsnorm(x, g):
    xf = x.astype(jnp.float32)
    y = xf * lax.rsqrt(jnp.mean(xf * xf, axis=-1, keepdims=True) + EPS)
    return (y * g.astype(jnp.float32)).astype(x.dtype)

def layernorm(x, g, b):
    xf = x.astype(jnp.float32)
    mu = jnp.mean(xf, axis=-1, keepdims=True)
    xc = xf - mu
    y = xc * lax.rsqrt(jnp.mean(xc * xc, axis=-1, keepdims=True) + EPS)
    return (y * g.astype(jnp.float32) + b.astype(jnp.float32)).astype(x.dtype)

def alibi_slopes(n):
    return jnp.exp2(-8.0 * jnp.arange(1, n + 1, dtype=jnp.float32) / n)

def mixer_projections(x, norm_g, w_in, q_norm_g, k_norm_g):
    h = rmsnorm(x, norm_g)
    p = h @ w_in
    q, k, v, ua, ub = jnp.split(p, [D_ATTN, D_ATTN + KV_DIM, D_ATTN + 2 * KV_DIM, D_ATTN + 2 * KV_DIM + D_CONV], axis=-1)
    lead = x.shape[:-1]
    q = rmsnorm(q.reshape(*lead, N_HEADS, HEAD_DIM), q_norm_g)
    k = rmsnorm(k.reshape(*lead, N_KV_HEADS, HEAD_DIM), k_norm_g)
    v = v.reshape(*lead, N_KV_HEADS, HEAD_DIM)
    u = ua * jax.nn.sigmoid(ub)
    return q, k, v, u

def swa_attend(q, k, v, q_pos, k_pos, sinks):
    *lead, tq, h, d = q.shape
    kvh = k.shape[-2]
    g = h // kvh
    qg = q.reshape(*lead, tq, kvh, g, d)
    s = jnp.einsum('...qhgd,...shd->...hgqs', qg, k).astype(jnp.float32) * (d ** -0.5)
    dist = q_pos[..., :, None] - k_pos[..., None, :]
    mask = (dist >= 0) & (dist < WINDOW) & (k_pos[..., None, :] >= 0)
    slopes = alibi_slopes(h).reshape(kvh, g, 1, 1)
    s = s - slopes * dist[..., None, None, :, :].astype(jnp.float32)
    s = jnp.where(mask[..., None, None, :, :], s, NEG_INF)
    sink = sinks.astype(jnp.float32).reshape(kvh, g, 1, 1)
    m = jnp.maximum(jnp.max(s, axis=-1, keepdims=True), sink)
    p = jnp.exp(s - m)
    denom = jnp.sum(p, axis=-1, keepdims=True) + jnp.exp(sink - m)
    o = jnp.einsum('...hgqs,...shd->...qhgd', (p / denom).astype(v.dtype), v)
    return o.reshape(*lead, tq, h * d)

def swa_prompt(q, k, v, sinks):
    b, s = q.shape[:2]
    nb = s // BLOCK
    qb = q.reshape(b, nb, BLOCK, N_HEADS, HEAD_DIM)
    kb = k.reshape(b, nb, BLOCK, N_KV_HEADS, HEAD_DIM)
    vb = v.reshape(b, nb, BLOCK, N_KV_HEADS, HEAD_DIM)
    pad = ((0, 0), (1, 0), (0, 0), (0, 0), (0, 0))
    k_band = jnp.concatenate([jnp.pad(kb[:, :-1], pad), kb], axis=2)
    v_band = jnp.concatenate([jnp.pad(vb[:, :-1], pad), vb], axis=2)
    starts = jnp.arange(nb, dtype=jnp.int32)[:, None] * BLOCK
    q_pos = starts + jnp.arange(BLOCK, dtype=jnp.int32)[None, :]
    k_pos = starts - BLOCK + jnp.arange(2 * BLOCK, dtype=jnp.int32)[None, :]
    o = swa_attend(qb, k_band, v_band, q_pos, k_pos, sinks)
    return o.reshape(b, s, D_ATTN)

def conv_module(u, past, dw_w, dw_b, ln_g, ln_b):
    full = jnp.concatenate([past, u], axis=1)
    y = lax.conv_general_dilated(full, dw_w[:, None, :], window_strides=(1,), padding='VALID',
                                 dimension_numbers=('NWC', 'WIO', 'NWC'), feature_group_count=D_CONV)
    y = jax.nn.silu(layernorm(y + dw_b, ln_g, ln_b))
    return y, full[:, -(CONV_WIDTH - 1):]

def memory_kv(mem, norm_mem_g, w_mk, w_mv, mk_norm_g):
    h = rmsnorm(mem, norm_mem_g)
    n, m = mem.shape[:2]
    k = rmsnorm((h @ w_mk).reshape(n, m, MEM_HEADS, MEM_HEAD_DIM), mk_norm_g)
    v = (h @ w_mv).reshape(n, m, MEM_HEADS, MEM_HEAD_DIM)
    return k, v

def cross_attend(x, mem_k, mem_v, norm_xa_g, w_mq, mq_norm_g, w_mo):
    h = rmsnorm(x, norm_xa_g)
    n, t = x.shape[:2]
    q = rmsnorm((h @ w_mq).reshape(n, t, MEM_HEADS, MEM_HEAD_DIM), mq_norm_g)
    s = jnp.einsum('nqhd,nmhd->nhqm', q, mem_k).astype(jnp.float32) * (MEM_HEAD_DIM ** -0.5)
    p = jax.nn.softmax(s, axis=-1).astype(mem_v.dtype)
    o = jnp.einsum('nhqm,nmhd->nqhd', p, mem_v).reshape(n, t, MEM_HEADS * MEM_HEAD_DIM)
    return o @ w_mo

def hier_moe(h, w_rg, b_rg, w_re, b_re, w_gate, w_up, w_down):
    shp = h.shape
    t = h.reshape(-1, D_MODEL)
    lg = (t @ w_rg).astype(jnp.float32) + b_rg.astype(jnp.float32)
    pg = jax.nn.softmax(lg, axis=-1)
    gsel = jnp.argmax(lg, axis=-1)
    pg_sel = jnp.take_along_axis(pg, gsel[:, None], axis=-1)
    le = ((t @ w_re).astype(jnp.float32) + b_re.astype(jnp.float32)).reshape(-1, N_GROUPS, EXPERTS_PER_GROUP)
    le_sel = jnp.take_along_axis(le, gsel[:, None, None], axis=1)[:, 0]
    top_v, top_i = lax.top_k(le_sel, TOP_K)
    gate = jax.nn.softmax(top_v, axis=-1) * pg_sel
    eidx = gsel[:, None] * EXPERTS_PER_GROUP + top_i
    comb = jnp.einsum('tk,tke->te', gate, jax.nn.one_hot(eidx, N_EXPERTS, dtype=jnp.float32))
    a = jnp.einsum('td,edf->tef', t, w_gate)
    b = jnp.einsum('td,edf->tef', t, w_up)
    act = jax.nn.silu(a) * b * comb[:, :, None].astype(t.dtype)
    y = jnp.einsum('tef,efd->td', act, w_down)
    return y.reshape(shp)

def layer_tail(x, attn, conv, mem_k, mem_v, w_out, norm_xa_g, w_mq, mq_norm_g, w_mo,
               norm_ffn_g, w_rg, b_rg, w_re, b_re, w_gate, w_up, w_down):
    x = x + jnp.concatenate([attn, conv], axis=-1) @ w_out
    x = x + cross_attend(x, mem_k, mem_v, norm_xa_g, w_mq, mq_norm_g, w_mo)
    x = x + hier_moe(rmsnorm(x, norm_ffn_g), w_rg, b_rg, w_re, b_re, w_gate, w_up, w_down)
    return x

def setup_inputs(seed: int = 0) -> dict:
    key = jax.random.key(seed)
    ks = iter(jax.random.split(key, 40))
    f32 = jnp.float32

    def nrm(shape, scale):
        return jax.random.normal(next(ks), shape, f32) * scale

    def gain(shape):
        return 1.0 + nrm(shape, 0.01)

    w_buf = min(WINDOW, PAST_LEN)
    return {
        'x_prompt': nrm((BATCH, SEQ, D_MODEL), 1.0),
        'x_sample': nrm((DEC_BATCH, DEC_SEQ, D_MODEL), 1.0),
        'cache_swa_k': nrm((DEPTH, DEC_BATCH, w_buf, N_KV_HEADS, HEAD_DIM), 1.0),
        'cache_swa_v': nrm((DEPTH, DEC_BATCH, w_buf, N_KV_HEADS, HEAD_DIM), 1.0),
        'state_conv': nrm((DEPTH, DEC_BATCH, CONV_WIDTH - 1, D_CONV), 0.5),
        'cache_mem_k': nrm((DEPTH, DEC_BATCH, MEM_LEN, MEM_HEADS, MEM_HEAD_DIM), 1.0),
        'cache_mem_v': nrm((DEPTH, DEC_BATCH, MEM_LEN, MEM_HEADS, MEM_HEAD_DIM), 1.0),
        'mem_prompt': nrm((BATCH, MEM_LEN, D_MODEL), 1.0),
        'norm_mix_g': gain((DEPTH, D_MODEL)),
        'w_in': nrm((DEPTH, D_MODEL, D_IN), D_MODEL ** -0.5),
        'q_norm_g': gain((DEPTH, HEAD_DIM)),
        'k_norm_g': gain((DEPTH, HEAD_DIM)),
        'attn_sinks': nrm((DEPTH, N_HEADS), 0.5),
        'conv_dw_w': nrm((DEPTH, CONV_WIDTH, D_CONV), CONV_WIDTH ** -0.5),
        'conv_dw_b': nrm((DEPTH, D_CONV), 0.01),
        'conv_ln_g': gain((DEPTH, D_CONV)),
        'conv_ln_b': nrm((DEPTH, D_CONV), 0.01),
        'w_out': nrm((DEPTH, D_ATTN + D_CONV, D_MODEL), (D_ATTN + D_CONV) ** -0.5),
        'norm_xa_g': gain((DEPTH, D_MODEL)),
        'norm_mem_g': gain((DEPTH, D_MODEL)),
        'w_mq': nrm((DEPTH, D_MODEL, MEM_HEADS * MEM_HEAD_DIM), D_MODEL ** -0.5),
        'w_mk': nrm((DEPTH, D_MODEL, MEM_HEADS * MEM_HEAD_DIM), D_MODEL ** -0.5),
        'w_mv': nrm((DEPTH, D_MODEL, MEM_HEADS * MEM_HEAD_DIM), D_MODEL ** -0.5),
        'mq_norm_g': gain((DEPTH, MEM_HEAD_DIM)),
        'mk_norm_g': gain((DEPTH, MEM_HEAD_DIM)),
        'w_mo': nrm((DEPTH, MEM_HEADS * MEM_HEAD_DIM, D_MODEL), (MEM_HEADS * MEM_HEAD_DIM) ** -0.5),
        'norm_ffn_g': gain((DEPTH, D_MODEL)),
        'w_router_group': nrm((DEPTH, D_MODEL, N_GROUPS), D_MODEL ** -0.5),
        'b_router_group': nrm((DEPTH, N_GROUPS), 0.01),
        'w_router_expert': nrm((DEPTH, D_MODEL, N_EXPERTS), D_MODEL ** -0.5),
        'b_router_expert': nrm((DEPTH, N_EXPERTS), 0.01),
        'w_exp_gate': nrm((DEPTH, N_EXPERTS, D_MODEL, D_EXPERT), D_MODEL ** -0.5),
        'w_exp_up': nrm((DEPTH, N_EXPERTS, D_MODEL, D_EXPERT), D_MODEL ** -0.5),
        'w_exp_down': nrm((DEPTH, N_EXPERTS, D_EXPERT, D_MODEL), D_EXPERT ** -0.5),
    }

def reference(x_prompt, x_sample, cache_swa_k, cache_swa_v, state_conv, cache_mem_k, cache_mem_v, mem_prompt,
              norm_mix_g, w_in, q_norm_g, k_norm_g, attn_sinks, conv_dw_w, conv_dw_b, conv_ln_g, conv_ln_b, w_out,
              norm_xa_g, norm_mem_g, w_mq, w_mk, w_mv, mq_norm_g, mk_norm_g, w_mo,
              norm_ffn_g, w_router_group, b_router_group, w_router_expert, b_router_expert,
              w_exp_gate, w_exp_up, w_exp_down):
    xp = x_prompt
    xs = x_sample
    w_buf = cache_swa_k.shape[2]
    wp = min(WINDOW, xp.shape[1])
    s_pos = PAST_LEN + jnp.arange(xs.shape[1], dtype=jnp.int32)
    kv_pos = jnp.concatenate([PAST_LEN - w_buf + jnp.arange(w_buf, dtype=jnp.int32), s_pos])
    kp_l, vp_l, cp_l, mkp_l, mvp_l, ks_l, vs_l, cs_l = [], [], [], [], [], [], [], []
    for l in range(DEPTH):
        tail = (w_out[l], norm_xa_g[l], w_mq[l], mq_norm_g[l], w_mo[l], norm_ffn_g[l],
                w_router_group[l], b_router_group[l], w_router_expert[l], b_router_expert[l],
                w_exp_gate[l], w_exp_up[l], w_exp_down[l])
        conv_p = (conv_dw_w[l], conv_dw_b[l], conv_ln_g[l], conv_ln_b[l])

        q, k, v, u = mixer_projections(xp, norm_mix_g[l], w_in[l], q_norm_g[l], k_norm_g[l])
        attn = swa_prompt(q, k, v, attn_sinks[l])
        conv0 = jnp.zeros((xp.shape[0], CONV_WIDTH - 1, D_CONV), u.dtype)
        conv, conv_new = conv_module(u, conv0, *conv_p)
        mk, mv = memory_kv(mem_prompt, norm_mem_g[l], w_mk[l], w_mv[l], mk_norm_g[l])
        xp = layer_tail(xp, attn, conv, mk, mv, *tail)
        kp_l.append(k[:, -wp:])
        vp_l.append(v[:, -wp:])
        cp_l.append(conv_new)
        mkp_l.append(mk)
        mvp_l.append(mv)

        q, k, v, u = mixer_projections(xs, norm_mix_g[l], w_in[l], q_norm_g[l], k_norm_g[l])
        k_all = jnp.concatenate([cache_swa_k[l], k], axis=1)
        v_all = jnp.concatenate([cache_swa_v[l], v], axis=1)
        attn = swa_attend(q, k_all, v_all, s_pos, kv_pos, attn_sinks[l])
        conv, conv_new = conv_module(u, state_conv[l], *conv_p)
        xs = layer_tail(xs, attn, conv, cache_mem_k[l], cache_mem_v[l], *tail)
        ks_l.append(k_all[:, -w_buf:])
        vs_l.append(v_all[:, -w_buf:])
        cs_l.append(conv_new)

    swa_k_prompt = jnp.stack(kp_l, axis=0)
    swa_v_prompt = jnp.stack(vp_l, axis=0)
    conv_prompt = jnp.stack(cp_l, axis=0)
    mem_k_prompt = jnp.stack(mkp_l, axis=0)
    mem_v_prompt = jnp.stack(mvp_l, axis=0)
    swa_k_sample = jnp.stack(ks_l, axis=0)
    swa_v_sample = jnp.stack(vs_l, axis=0)
    conv_sample = jnp.stack(cs_l, axis=0)
    return (xp, xs, swa_k_prompt, swa_v_prompt, conv_prompt, mem_k_prompt, mem_v_prompt,
            swa_k_sample, swa_v_sample, conv_sample)


_drawn_inputs = setup_inputs


def setup_inputs(seed=0):
    import zlib

    import numpy as np

    out = dict(_drawn_inputs(seed))
    spreads = {}
    factors = {'norm_mix_g': 3.624,
     'q_norm_g': 6.771,
     'k_norm_g': 5.48,
     'attn_sinks': 24.12,
     'conv_ln_g': 4.136,
     'conv_ln_b': 3.586,
     'norm_xa_g': 3.712,
     'norm_mem_g': 5.674,
     'mq_norm_g': 8.0,
     'mk_norm_g': 5.332,
     'b_router_group': 51.848,
     'conv_dw_b': 3.653,
     'norm_ffn_g': 5.29,
     'b_router_expert': 5.786}
    for name, (base, spread) in spreads.items():
        noise = np.random.default_rng([zlib.crc32(name.encode()), seed]).standard_normal(out[name].shape)
        drawn = base * np.exp(spread * noise) if base else spread * noise
        out[name] = jnp.asarray(drawn.astype(out[name].dtype))
    for name, factor in factors.items():
        out[name] = (out[name] * factor).astype(out[name].dtype)
    return out
```

```python
import numpy as np
import concourse.bass as bass
from concourse import mybir
from contextlib import ExitStack

D = 1024
DC = D // 128
SEQ, DEC_B, DEC_T = 1024, 8, 8
NS = DEC_B * DEC_T
NTOK = SEQ + NS
HEADS, HD, KVH = 8, 64, 2
CONV, TAPS = 512, 31
CC = CONV // 128
PAST = TAPS - 1
DIN = 512 + 2 * 128 + 2 * CONV
MEM, MH, MHD = 256, 4, 256
NG, EPG = 4, 8
NE, FE = 32, 256
NT = 9
OVER = 16
NSLOT = NE + OVER
EPS = 1e-6
MASKED = 1e30
SCALE, MSCALE = HD ** -0.5, MHD ** -0.5

CONSTS = [("ident", 128), ("mean", 128), ("dist", 256), ("dist_s", 192), ("tri", 128), ("ones", 128),
          ("iota", 128), ("tri33", 33), ("tok", NT), ("thr", 8), ("o16", OVER)]
CAT = {}
_at = 0
for _n, _w in CONSTS:
    CAT[_n] = (_at, _at + _w)
    _at += _w
NCONST = _at


def shape_constants():
    c = np.zeros((128, NCONST), np.float32)
    p = np.arange(128)

    def put(name, v):
        c[:v.shape[0], CAT[name][0]:CAT[name][1]] = v
    put("ident", np.eye(128))
    put("mean", np.full((128, 128), 1.0 / CONV))
    d = p[:, None] + 128 - np.arange(256)[None, :]
    put("dist", np.where((d >= 0) & (d < 128), d, MASKED))
    t = np.arange(NS)
    dc = 128 + (t % DEC_T)[:, None] - np.arange(128)[None, :]
    dn = (t % DEC_T)[:, None] - (t % DEC_T)[None, :]
    same = (t // DEC_T)[:, None] == (t // DEC_T)[None, :]
    put("dist_s", np.concatenate([np.where(dc < 128, dc, MASKED), np.where(same & (dn >= 0), dn, MASKED)], 1))
    put("tri", (p[:, None] < p[None, :]) * 1.0)
    put("ones", np.ones((128, 128)))
    put("iota", np.tile(p[None, :], (128, 1)))
    put("tri33", (np.arange(32)[:, None] < np.arange(33)[None, :]) * 1.0)
    tok = np.zeros((128, NT))
    tok[:NS, 0] = SEQ + t
    for s in range(1, NT):
        tok[:, s] = (s - 1) * 128 + p
    put("tok", tok)
    put("thr", np.tile(128.0 * np.arange(1, 9)[None, :], (128, 1)))
    put("o16", np.tile(np.arange(OVER)[None, :], (128, 1)))
    return c


def rows_of(s):
    return NS if s == 0 else 128


def build(nc, i, o):
    f32 = mybir.dt.float32
    i32 = mybir.dt.int32
    ALU = mybir.AluOpType
    ACT = mybir.ActivationFunctionType
    X = mybir.AxisListType.X
    ctx = ExitStack()
    with ctx:
        def sb(name, cols, dt=f32, rows=128):
            return ctx.enter_context(nc.sbuf_tensor(name, [rows, cols], dt))

        def sem(name):
            return ctx.enter_context(nc.semaphore(name))

        W = sb("W", 38912)
        RIN, ROUT, RMQ, RMO = 0, 14336, 22528, 30720
        G = sb("G", 12800)
        cst = sb("cst", 256)
        ident, meanw = cst[:, 0:128], cst[:, 128:256]
        cvec = sb("cvec", 48)
        gk_bc = sb("gk_bc", 64)
        sink_bc = sb("sink_bc", 8)
        sink8 = sb("sink8", 8)
        br_bc = sb("br_bc", 36)
        dwT = sb("dwT", CC * TAPS)
        LG = sb("LG", NT * 36)
        WR = sb("WR", DC * 36)
        gates = sb("gates", 2 * NT)
        idxs = sb("idxs", 4, i32)
        slot_i = sb("slot_i", 2 * NT, i32)
        idx_i = sb("idx_i", NSLOT, i32)
        eid_i = sb("eid_i", OVER + 1, i32)
        mhalf = sb("mhalf", 1)
        st = sb("st", 96)

        def view(base, off, *dims):
            n = int(np.prod(dims))
            v = base[:, off:off + n]
            if len(dims) == 2:
                return v.rearrange("p (a b) -> p a b", a=dims[0])
            if len(dims) == 3:
                return v.rearrange("p (a b c) -> p a b c", a=dims[0], b=dims[1])
            if len(dims) == 4:
                return v.rearrange("p (a b c d) -> p a b c d", a=dims[0], b=dims[1], c=dims[2])
            return v

        w_in = view(W, RIN, DC, DIN)
        w_out = view(W, ROUT, DC, D)
        w_mv = view(W, ROUT, DC, D)
        w_mk = view(W, RMQ, DC, D)
        w_mq = view(W, RMQ, DC, D)
        w_mo = view(W, RMO, DC, D)
        MKT = view(G, 0, DC, MEM)
        MV = view(G, 2048, 2, D)
        XR = [view(G, 4096 + 1024 * r, D) for r in range(4)]
        Z = view(G, 8192, D)
        HT = view(G, 9216, DC, 128)
        QN = view(G, 10240, 512)
        QT = view(G, 10752, 4, 128)
        KT = [view(G, 11264 + 128 * r, 128) for r in range(3)]
        VV = [view(G, 11648 + 128 * r, 128) for r in range(3)]
        KN = view(G, 12032, 128)
        TMP = view(G, 12160, 512)
        LND = view(G, 12672, 128)
        S = view(W, RMO, HEADS, 256)
        PT = view(W, RMO + 2048, 2, HEADS, 128)
        PTS = view(W, RMO + 2048, 2, HEADS, NS)
        OT = view(W, RMO + 4096, 4, 128)
        CT = view(W, RMO + 4608, CC, 128)
        UT = [view(W, RMO + 5120 + 640 * r, CC, 160) for r in range(2)]
        UTS = view(W, RMO + 5120, CC, DEC_B, PAST + DEC_T)
        Y = [view(W, RMO + 6400, CC, NS if r == 0 else 128) if r == 0 else view(W, RMO + 6400 + 512 * (r % 2), CC, 128) for r in range(NT)]
        U = view(W, RMO + 7424, 512)
        DIST = view(W, RMO + 7936, 256)
        JUNK = view(W, RMO, D)
        MK_N = view(W, RMO + 1024, MH, MHD)
        GMK = view(W, RMO + 2048, MHD)
        STAGE = view(W, RMO + 2304, 128)
        DWS = view(W, RMO + 2432, CONV)
        SK = view(W, RMQ, DEC_B, 128)
        SV = view(W, RMQ + 1024, DEC_B, 128)
        SKT = view(W, RMQ + 2048, DEC_B, 128)
        QP = view(W, RMQ + 3072, DEC_B, 4, NS)
        SST = view(W, RMQ + 5120, 2, CONV)
        DIST_S = view(W, RMQ + 6144, 192)
        QN2 = view(G, 10240, MH, MHD)
        QT2 = view(G, 11264, DC, 128)
        S2 = view(W, ROUT, MH, MEM)
        PT2 = view(W, ROUT + 1024, 2, MH, 128)
        OT2 = view(W, ROUT + 2048, DC, 128)
        Z3 = view(W, ROUT + 3072, D)
        H3 = view(W, ROUT + 4096, DC, 128)
        SQ2 = view(W, ROUT + 5120, D)
        MKB = [view(W, RIN + 2048 * r, 2, D) for r in range(2)]
        MVB = [view(W, RIN + 4096 + 2048 * r, 2, D) for r in range(2)]
        MKTB = view(W, RIN + 8192, DC, MEM)
        QP2 = view(W, RIN + 10240, DEC_B, DC, NS)
        SQ3 = view(W, ROUT + 6144, D)
        RC = G[:, 0:NCONST - CAT["tri"][0]]
        def rc(name):
            lo = CAT[name][0] - CAT["tri"][0]
            return RC[:, lo:lo + CAT[name][1] - CAT[name][0]]
        tri, ones, iota, tri33, tok, thr, o16 = (rc(n) for n in ("tri", "ones", "iota", "tri33", "tok", "thr", "o16"))
        _r = [512]

        def rt(*dims):
            v = view(G, _r[0], *dims)
            _r[0] += int(np.prod(dims))
            return v
        down8, R_M1, R_M2, RT9, R_T9, R_PG, R_E2 = rt(8), rt(NT), rt(NT), rt(NT), rt(NT), rt(NT), rt(NT)
        R_OG, R_K4, R_EG = rt(NT, NG), rt(NT, NG), rt(NT, NG)
        R_SEL, R_T8, R_K8, R_O1, R_O2 = (rt(NT, EPG) for _ in range(5))
        RO, RP3 = rt(2 * NT, NE), rt(2 * NT, NE)
        RM3, RA3 = rt(NT, NE), rt(NT, NE)
        RM, RA = RM3.rearrange("p t e -> p (t e)"), RA3.rearrange("p t e -> p (t e)")
        RTOT, R_CNT, R_GT, ROV, RBASE = rt(NE), rt(1), rt(8), rt(128), rt(33)
        R_RANK, R_EXP, R_BASE, R_FL, R_ROW = (rt(2 * NT) for _ in range(5))
        RG8, RE3, R_EID = rt(2 * NT, 8), rt(OVER, NE), rt(OVER)
        RR, RQ = view(G, 9216, 2 * NT, 128), view(G, 11520, 2 * NT, NSLOT)
        SLOT = [0, 6144, RMQ, RMO]
        WGU = [view(W, a, DC, 2 * FE) for a in SLOT]
        WD = [view(W, a + 4096, 2, D) for a in SLOT]
        ZG = [view(W, ROUT + 1024 * r, D) for r in range(2)]
        HG = [view(W, ROUT + 2048 + 1024 * r, DC, 128) for r in range(2)]
        YB = [view(W, ROUT + 4096 + 1024 * r, D) for r in range(2)]
        EB = [view(W, ROUT + 6144 + 256 * r, FE) for r in range(2)]
        AB = [view(W, ROUT + 6656 + 256 * r, FE) for r in range(2)]
        AT = [view(W, ROUT + 7168 + 256 * r, 2, 128) for r in range(2)]
        CX = [view(W, RIN + 1024 * r, D) for r in range(2)]
        CY = [view(W, RIN + 2048 + 1024 * r, D) for r in range(4)]
        CO = [view(W, RIN + 6144 + 1024 * r, D) for r in range(2)]

        B = [ctx.enter_context(nc.psum_tensor(f"bank{k}", [128, 512], f32)) for k in range(8)]

        x1_d = nc.dram_tensor("x1_scratch", [NTOK, D], f32).ap()
        x2_d = nc.dram_tensor("x2_scratch", [NTOK, D], f32).ap()
        z3_d = nc.dram_tensor("z3_scratch", [NTOK, D], f32).ap()
        y_d = nc.dram_tensor("y_scratch", [NSLOT * 128, D], f32).ap()

        xs_flat = i["x_sample"].rearrange("b t d -> (b t) d")
        xp_flat = i["x_prompt"].rearrange("b t d -> (b t) d")

        def tok_rows(t, s):
            return t[SEQ:NTOK, :] if s == 0 else t[(s - 1) * 128:s * 128, :]

        def x_rows(s):
            return xs_flat if s == 0 else xp_flat[(s - 1) * 128:s * 128, :]

        V_MIX, V_XA, V_MEM, V_FFN, V_DWB, V_LNG, V_LNB, V_GQ, V_MQ = 0, 8, 16, 24, 32, 36, 40, 44, 45
        NV = 47

        def ring(name, n):
            return [sem(f"{name}{r}") for r in range(n)]

        M = {n: sem(n) for n in """c_in small_in wmk_in wmv_in win_in wout_in wmq_in wmo_in dist_in wr_in skv_in rconst_in
            moved_out vec_tdone vec_ready mhalf_ready mean_eps
            x_sq x_rs z_ready zt_done ht_ready
            mk_done mv_done mk_sq mk_ssq mk_rs mk_normed mkn_ready mv_ready mkt_done mktA_ready mktD_ready mem_out
            pq_done pub_done qn_ready kn_ready v_ready kvu_out
            ub_exp u_ready qT_done uT_done kT_done qT_ready uT_ready kT_ready
            skt_done skt_ready qp_zero qp_ready sst_done sst_ready
            sc_done s_ready nm_ready s_exp p_ready ptA_done ptD_done ptA_ready ptD_ready pvA_done pvD_done otA_ready otD_ready
            conv_tap halo ln1_done xc_ready ln_sq ln_diag ln3_done ln2_done lnr_ready ln_rs v_act ln_exp ct_ready wo_done x1_ready
            mkb_used mvb_used
            z3_sq z3_rs z3_ready z3_out z3t_done h3_ready rt_done lg_ready
            r_arg r_exp ex_chain r_pref route_ready
            idx_copied gather_go zt4_done hg_ready gu_done gu_exp ab_ready at_done at_ready dn_done yb_readyA yb_readyD
            co_ready co_done dve""".split()}
        AFTER, ALIAS = {}, {}
        for name, (first, count) in {
            "q2_sq": ("qk_sq", 4 + 2 * NT),
            "q2_ssq": ("qk_ssq", 2 + 2 * NT),
            "q2_rs": ("qk_rs", 2 + NT),
            "q2n_ready": ("qn_ready", NT),
            "q2T_done": ("qT_done", NT),
            "q2T_ready": ("qT_ready", NT),
            "sc2_done": ("sc_done", 4 * NT),
            "s2_exp": ("s_exp", 9 * NT),
            "nm2_ready": ("nm_ready", NT),
            "p2_ready": ("p_ready", NT),
            "pt2A_done": ("ptA_done", 2 * NT - 1),
            "pt2D_done": ("ptD_done", 2 * NT - 1),
            "pt2A_ready": ("ptA_ready", 2 * NT - 1),
            "pt2D_ready": ("ptD_ready", 2 * NT - 1),
            "pv2A_done": ("pvA_done", NT),
            "pv2D_done": ("pvD_done", NT),
            "ot2A_ready": ("otA_ready", NT),
            "ot2D_ready": ("otD_ready", NT),
            "mo_done": ("wo_done", 2 * NT),
            "x2_ready": ("x1_ready", 2 * NT),
            "mq_done": ("pq_done", NT),
            "qk_sq": ("mk_sq", 4),
            "qk_ssq": ("mk_ssq", 2),
            "qk_rs": ("mk_rs", 2),
            "pkv_done": ("mk_done", 4),
            "pua_done": ("mv_done", 4),
            "mkbA_ready": ("skt_ready", 2),
            "mkb_tA": ("skt_done", 2),
            "mkb_tD": ("sst_done", 2),
            "mkbD_ready": ("halo", NT - 1),
            "qp2_ready": ("qp_ready", DEC_B),
            "qp2_zero": ("qp_zero", 1),
            "r_mask": ("r_arg", 2),
            "r_ov": ("r_arg", 3),
            "r_rows": ("r_arg", 4),
            "r_base": ("r_pref", 1),
            "r_table": ("r_pref", 2),
            "over_t": ("zt4_done", 2 * NE),
            "over_h": ("hg_ready", 2 * NE),
            "over_gu": ("gu_done", NE),
            "over_e": ("gu_exp", NE),
            "over_at": ("at_done", NE),
            "over_atr": ("at_ready", NE),
            "over_dn": ("dn_done", 2 * NE),
            "over_yA": ("yb_readyA", NE),
            "over_yD": ("yb_readyD", NE),
            "over_idx": ("idx_copied", NE // 4 - 1),
        }.items():
            AFTER[name] = count
            ALIAS[name] = first
        for name, first in ALIAS.items():
            while first in ALIAS:
                first = ALIAS[first]
            M[name] = M[first]
        x_in, x1_in, x1_out, x2_out = ring("x_in", 4), ring("x1_in", 4), ring("x1_out", 4), ring("x2_out", 4)
        mk_in, mv_in = ring("mkb_in", 2), ring("mvb_in", 2)
        wexp_in, zg_in, y_out = ring("wexp_in", 4), ring("zg_in", 2), ring("y_out", 2)
        cx_in, cy_in, co_out = ring("cx_in", 2), ring("cy_in", 4), ring("co_out", 2)

        def bc(ap, n, axis):
            if axis == 2:
                return ap[:, :, None].to_broadcast([ap.shape[0], ap.shape[1], n])
            return ap[:, None, :].to_broadcast([ap.shape[0], n, ap.shape[1]])

        def key_range(s):
            return (0, 192) if s == 0 else (128, 256) if s == 1 else (0, 256)

        def load_expert(eng, e, u, landed):
            if isinstance(e, int):
                g, up, dn = i["w_exp_gate"][0, e], i["w_exp_up"][0, e], i["w_exp_down"][0, e]
            else:
                g, up, dn = (i[n][0, bass.ds(e, 1)].rearrange("o a b -> (o a) b")
                             for n in ("w_exp_gate", "w_exp_up", "w_exp_down"))
            eng.dma_start(WGU[u][:, :, 0:FE], g.rearrange("(c p) n -> p c n", p=128)).then_inc(landed, 16)
            eng.dma_start(WGU[u][:, :, FE:2 * FE], up.rearrange("(c p) n -> p c n", p=128)).then_inc(landed, 16)
            eng.dma_start(WD[u], dn.rearrange("(c p) n -> p c n", p=128)).then_inc(landed, 16)

        def load_rows(eng, dst, src, landed):
            rows = src.rearrange("(c p) n -> p c n", p=128)
            for c in range(0, DC, 2):
                eng.dma_start(dst[:, c:c + 2, :], rows[:, c:c + 2, :]).then_inc(landed, 16)

        def store_out(sp, s):
            sp.wait_ge(M["co_ready"], s + 1)
            dst = o["y_s"].rearrange("b t d -> (b t) d") if s == 0 else o["y_p"][0, (s - 1) * 128:s * 128, :]
            sp.dma_start(dst, CO[s % 2][0:rows_of(s), :]).then_inc(co_out[s % 2], 16)

        block = ctx.enter_context(nc.Block())

        @block.sync
        def _(sp):
            kc = i["consts"]
            sp.dma_start(cst[:, :], kc[:, 0:256]).then_inc(M["c_in"], 16)
            small = 0
            r = 0
            for name, n in (("norm_mix_g", 8), ("norm_xa_g", 8), ("norm_mem_g", 8), ("norm_ffn_g", 8),
                            ("conv_dw_b", 4), ("conv_ln_g", 4), ("conv_ln_b", 4)):
                sp.dma_start(STAGE[r:r + n, :], i[name][0].rearrange("(c p) -> c p", p=128)).then_inc(M["small_in"], 16)
                r += n
            for half in range(2):
                sp.dma_start(STAGE[V_GQ:V_GQ + 1, 64 * half:64 * half + 64], i["q_norm_g"]).then_inc(M["small_in"], 16)
            sp.dma_start(STAGE[V_MQ:V_MQ + 2, :], i["mq_norm_g"][0].rearrange("(c p) -> c p", p=128)).then_inc(M["small_in"], 16)
            sp.dma_start(DWS[0:TAPS, :], i["conv_dw_w"][0]).then_inc(M["small_in"], 16)
            for dst, name, n in ((GMK, "mk_norm_g", MHD), (gk_bc[:, :], "k_norm_g", HD), (sink_bc[:, :], "attn_sinks", HEADS),
                                 (br_bc[:, 0:NG], "b_router_group", NG), (br_bc[:, NG:36], "b_router_expert", NE)):
                sp.dma_start(dst, i[name].to_broadcast([128, n])).then_inc(M["small_in"], 16)
            mem = i["mem_prompt"][0]
            for m in range(2):
                sp.dma_start(XR[m], mem[m * 128:(m + 1) * 128, :]).then_inc(x_in[m], 16)
            load_rows(sp, w_mk, i["w_mk"][0], M["wmk_in"])
            load_rows(sp, w_mv, i["w_mv"][0], M["wmv_in"])
            for s in range(2):
                sp.dma_start(XR[s + 2][0:rows_of(s), :], x_rows(s)).then_inc(x_in[s + 2], 16)
            load_rows(sp, w_in, i["w_in"][0], M["win_in"])
            wr = view(WR, 0, DC, 36)
            sp.dma_start(wr[:, :, 0:NG], i["w_router_group"][0].rearrange("(c p) n -> p c n", p=128)).then_inc(M["wr_in"], 16)
            sp.dma_start(wr[:, :, NG:36], i["w_router_expert"][0].rearrange("(c p) n -> p c n", p=128)).then_inc(M["wr_in"], 16)
            sp.wait_ge(M["mk_done"], 4)
            sp.dma_start(SK, i["cache_swa_k"][0].rearrange("b s h d -> s b (h d)")).then_inc(M["skv_in"], 16)
            sp.dma_start(SV, i["cache_swa_v"][0].rearrange("b s h d -> s b (h d)")).then_inc(M["skv_in"], 16)
            for g in range(2):
                sp.dma_start(SST[0:4 * PAST, g, :], i["state_conv"][0, 4 * g:4 * g + 4].rearrange("b t c -> (b t) c")).then_inc(M["skv_in"], 16)
            sp.dma_start(DIST_S[0:NS, :], kc[0:NS, CAT["dist_s"][0]:CAT["dist_s"][1]]).then_inc(M["skv_in"], 16)
            sp.wait_ge(M["mv_done"], 4)
            wo = i["w_out"][0]
            for kv in range(2):
                sp.dma_start(w_out[64 * kv:64 * kv + 64, 0:4, :],
                             wo[256 * kv:256 * kv + 256, :].rearrange("(j p) n -> p j n", p=64)).then_inc(M["wout_in"], 16)
            sp.dma_start(w_out[:, 4:8, :], wo[512:1024, :].rearrange("(c p) n -> p c n", p=128)).then_inc(M["wout_in"], 16)
            sp.dma_start(DIST, kc[:, CAT["dist"][0]:CAT["dist"][1]]).then_inc(M["dist_in"], 16)
            sp.wait_ge(M["dve"], 1)
            zeros = LG[:, None, 0:256].to_broadcast([128, OVER * 4, 256])
            sp.dma_start(y_d[NE * 128:, :].rearrange("(p n) (q d) -> p (n q) d", p=128, d=256), zeros).then_inc(M["moved_out"], 16)
            sp.dma_start(o["swa_k_s"][0, :, 0:128 - DEC_T], i["cache_swa_k"][0, :, DEC_T:128]).then_inc(M["moved_out"], 16)
            sp.dma_start(o["swa_v_s"][0, :, 0:128 - DEC_T], i["cache_swa_v"][0, :, DEC_T:128]).then_inc(M["moved_out"], 16)
            sp.dma_start(o["conv_s"][0, :, 0:PAST - DEC_T], i["state_conv"][0, :, DEC_T:PAST]).then_inc(M["moved_out"], 16)
            for it in range(NT + 2):
                s1, s3 = it, it - 2
                if s3 >= 0:
                    sp.wait_ge(M["x1_ready"], 2 * s3 + 2)
                    k = (s3 + 2) % 4
                    sp.dma_start(tok_rows(x1_d, s3), XR[k][0:rows_of(s3), :]).then_inc(x1_out[k], 16)
                if 2 <= it + 2 < NT:
                    k = it % 4
                    if s3 >= 0:
                        sp.wait_ge(x1_out[k], 16 * (s3 // 4 + 1))
                    else:
                        sp.wait_ge(M["z_ready"], it + 1)
                    sp.dma_start(XR[k], x_rows(it + 2)).then_inc(x_in[k], 16)
                if s1 == 0:
                    sp.wait_ge(M["kn_ready"], 1)
                    sp.wait_ge(M["v_ready"], 1)
                    sp.wait_ge(M["u_ready"], 1)
                    for b in range(DEC_B):
                        rows = slice(b * DEC_T, (b + 1) * DEC_T)
                        sp.dma_start(o["swa_k_s"][0, b, 128 - DEC_T:128].rearrange("t h d -> t (h d)"), KN[rows, :]).then_inc(M["kvu_out"], 16)
                        sp.dma_start(o["swa_v_s"][0, b, 128 - DEC_T:128].rearrange("t h d -> t (h d)"), VV[0][rows, :]).then_inc(M["kvu_out"], 16)
                        sp.dma_start(o["conv_s"][0, b, PAST - DEC_T:PAST], U[rows, :]).then_inc(M["kvu_out"], 16)
                if s1 == NT - 1:
                    sp.wait_ge(M["kn_ready"], NT)
                    sp.wait_ge(M["v_ready"], NT)
                    sp.wait_ge(M["u_ready"], NT)
                    sp.dma_start(o["swa_k_p"][0, 0].rearrange("t h d -> t (h d)"), KN).then_inc(M["kvu_out"], 16)
                    sp.dma_start(o["swa_v_p"][0, 0].rearrange("t h d -> t (h d)"), VV[(NT - 1) % 3]).then_inc(M["kvu_out"], 16)
                    sp.dma_start(o["conv_p"][0, 0], U[128 - PAST:128, :]).then_inc(M["kvu_out"], 16)
                    sp.wait_ge(M["pua_done"], AFTER["pua_done"] + NT)
                    for b in range(2):
                        sp.dma_start(MKB[b], i["cache_mem_k"][0, b].rearrange("(h p) e d -> p h (e d)", p=128)).then_inc(mk_in[b], 16)
                        sp.dma_start(MVB[b], i["cache_mem_v"][0, b].rearrange("(h p) e d -> p h (e d)", p=128)).then_inc(mv_in[b], 16)
                if s1 == 3:
                    sp.wait_ge(M["pvA_done"], 1)
                    sp.wait_ge(M["pvD_done"], 1)
                    sp.wait_ge(M["s_ready"], 8)
                    load_rows(sp, w_mq, i["w_mq"][0], M["wmq_in"])
                if s3 == 6 or s3 == 7:
                    s = s3 - 6
                    sp.wait_ge(x1_out[s], 32)
                    sp.dma_start(XR[s][0:rows_of(s), :], tok_rows(x1_d, s)).then_inc(x1_in[s], 16)
            sp.wait_ge(M["wo_done"], 2 * NT)
            sp.wait_ge(M["x_sq"], NT + 3)
            load_rows(sp, w_mo, i["w_mo"][0], M["wmo_in"])
            for b in range(2, DEC_B):
                sp.wait_ge(M["mkb_used"], b - 1)
                sp.dma_start(MKB[b % 2], i["cache_mem_k"][0, b].rearrange("(h p) e d -> p h (e d)", p=128)).then_inc(mk_in[b % 2], 16)
            for it in range(NT + 2):
                s1, s2, s3 = it, it - 1, it - 2
                if it == 0:
                    sp.wait_ge(x1_out[2], 48)
                if s3 >= 0:
                    sp.wait_ge(M["z3_ready"], s3 + 1)
                    sp.wait_ge(x2_out[s3 % 4], 16 * (s3 // 4 + 1))
                    sp.dma_start(tok_rows(z3_d, s3), Z3[0:rows_of(s3), :]).then_inc(M["z3_out"], 16)
                if 2 <= it + 2 < NT:
                    k = (it + 2) % 4
                    if it + 2 == 3:
                        sp.wait_ge(x1_out[3], 32)
                    sp.dma_start(XR[k], tok_rows(x1_d, it + 2)).then_inc(x1_in[k], 16)
                if s2 == 0:
                    for b in range(2, DEC_B):
                        sp.wait_ge(M["mvb_used"], b - 1)
                        sp.dma_start(MVB[b % 2], i["cache_mem_v"][0, b].rearrange("(h p) e d -> p h (e d)", p=128)).then_inc(mv_in[b % 2], 16)
                if 0 <= s2 < NT:
                    sp.wait_ge(M["x2_ready"], AFTER["x2_ready"] + 2 * s2 + 2)
                    sp.dma_start(tok_rows(x2_d, s2), XR[s2 % 4][0:rows_of(s2), :]).then_inc(x2_out[s2 % 4], 16)
                if s2 == 2:
                    sp.wait_ge(M["mvb_used"], DEC_B)
                    for e in range(2):
                        load_expert(sp, e, e, wexp_in[e])
                if s1 == NT - 1:
                    sp.wait_ge(M["mq_done"], AFTER["mq_done"] + 2 * NT)
                    load_expert(sp, 2, 2, wexp_in[2])
            sp.wait_ge(M["mo_done"], AFTER["mo_done"] + 2 * NT)
            load_expert(sp, 3, 3, wexp_in[3])
            r0 = CAT["tri"][0]
            sp.wait_ge(M["x2_ready"], AFTER["x2_ready"] + 2 * NT)
            sp.dma_start(RC, kc[:, r0:NCONST]).then_inc(M["rconst_in"], 16)

            def store_y(n, u):
                sp.wait_ge(M["yb_readyA"], n + 1)
                sp.wait_ge(M["yb_readyD"], n + 1)
                if isinstance(n, int):
                    dst = y_d[n * 128:(n + 1) * 128, :]
                else:
                    dst = y_d[bass.ds(n * 128, 128), :]
                sp.dma_start(dst, YB[u % 2]).then_inc(y_out[u % 2], 16)
            with sp.Fori(0, NE // 4 - 1) as it:
                for u in range(4):
                    store_y(it * 4 + u, u)
                    load_expert(sp, it * 4 + (u + 4), u, wexp_in[u])
            for u in range(4):
                store_y(NE - 4 + u, u)
            sp.wait_ge(M["dn_done"], 2 * NE)
            sp.wait_ge(M["moved_out"], 64)
            total = sp.value_load(eid_i[0:1, OVER:OVER + 1], min_val=0, max_val=OVER)
            with sp.Fori(0, OVER) as n:
                with sp.If(total > n):
                    e = sp.value_load(eid_i[0:1, bass.ds(n, 1)], min_val=0, max_val=NE - 1)
                    load_expert(sp, e, 0, wexp_in[0])
                    sp.wait_ge(M["over_yA"], AFTER["over_yA"] + n + 1)
                    sp.wait_ge(M["over_yD"], AFTER["over_yD"] + n + 1)
                    sp.dma_start(y_d[bass.ds(n * 128 + NE * 128, 128), :], YB[0]).then_inc(y_out[0], 16)
            for s in range(NT):
                if s >= 2:
                    sp.wait_ge(M["co_ready"], s - 1)
                sp.dma_start(CX[s % 2][0:rows_of(s), :], tok_rows(x2_d, s)).then_inc(cx_in[s % 2], 16)
                if s >= 1:
                    store_out(sp, s - 1)
            store_out(sp, NT - 1)
            sp.wait_ge(co_out[0], 16 * ((NT + 1) // 2))
            sp.wait_ge(co_out[1], 16 * (NT // 2))
            sp.wait_ge(M["moved_out"], 64)
            sp.wait_ge(M["kvu_out"], 16 * (3 * DEC_B + 3))
            sp.wait_ge(M["mem_out"], 64)

        @block.gpsimd
        def _(pool):
            pool.memset(mhalf[:, :], -0.5).then_inc(M["mhalf_ready"], 1)
            pool.wait_ge(M["mhalf_ready"], 1)

            means = [0]

            def rsqrt(src, dst, rs_sem, mul):
                pool.tensor_scalar(dst, src, mul, EPS, ALU.mult, ALU.add).then_inc(M["mean_eps"], 1)
                means[0] += 1
                pool.wait_ge(M["mean_eps"], means[0])
                half = mhalf[0:dst.shape[0], 0:1].to_broadcast([dst.shape[0], dst.shape[1]])
                pool.tensor_tensor(dst, dst, half, ALU.pow).then_inc(M[rs_sem], 1)

            def norm_x(n, rows):
                pool.wait_ge(M["x_sq"], n + 1)
                rsqrt(st[0:rows, n % 2:n % 2 + 1], st[0:rows, 2 + n % 2:3 + n % 2], "x_rs", 1.0 / D)

            norm_x(0, 128)
            pool.wait_ge(M["mk_ssq"], 1)
            rsqrt(st[:, 4:8], st[:, 8:12], "mk_rs", 1.0 / MHD)
            norm_x(1, 128)
            pool.wait_ge(M["mk_ssq"], 2)
            rsqrt(st[:, 4:8], st[:, 8:12], "mk_rs", 1.0 / MHD)
            norm_x(2, rows_of(0))
            pool.wait_ge(M["mk_done"], 4)
            pool.memset(QP, 0.0).then_inc(M["qp_zero"], 1)
            for it in range(NT + 2):
                s1, s2, s3 = it, it - 1, it - 2
                if s3 >= 0:
                    n = rows_of(s3)
                    pool.wait_ge(M["lnr_ready"], s3 + 1)
                    rsqrt(st[0:n, 90:91], st[0:n, 91:92], "ln_rs", 1.0)
                if s1 < NT:
                    n = rows_of(s1)
                    pool.wait_ge(M["qk_ssq"], AFTER["qk_ssq"] + 2 * s1 + 2)
                    rsqrt(st[0:n, 12:22], st[0:n, 22:32], "qk_rs", 1.0 / HD)
                if s1 + 1 < NT:
                    norm_x(s1 + 3, rows_of(s1 + 1))
            norm_x(NT + 2, rows_of(0))
            pool.memset(QP2, 0.0).then_inc(M["qp2_zero"], 1)
            for it in range(NT + 2):
                s1, s2, s3 = it, it - 1, it - 2
                if s3 >= 0:
                    n = rows_of(s3)
                    pool.wait_ge(M["z3_sq"], s3 + 1)
                    rsqrt(st[0:n, 40:41], st[0:n, 41:42], "z3_rs", 1.0 / D)
                if s1 < NT:
                    n = rows_of(s1)
                    pool.wait_ge(M["q2_ssq"], AFTER["q2_ssq"] + s1 + 1)
                    rsqrt(st[0:n, 32:36], st[0:n, 36:40], "q2_rs", 1.0 / MHD)
                if s1 + 1 < NT:
                    norm_x(s1 + NT + 3, rows_of(s1 + 1))

            def gather(col, landed, buf):
                pool.indirect_dma_start(out=buf, out_offset=None, in_=z3_d,
                                        in_offset=bass.IndirectOffsetOnAxis(ap=col, axis=0)).then_inc(landed, 16)

            pool.wait_ge(M["route_ready"], 1)
            pool.wait_ge(M["z3_out"], 16 * NT)
            for n in range(2):
                gather(idx_i[:, n:n + 1], zg_in[n], ZG[n])
            with pool.Fori(0, NE // 4 - 1) as it:
                pool.wait_ge(zg_in[0], it * 32 + 16)
                pool.wait_ge(zg_in[1], it * 32 + 16)
                pool.tensor_copy(idxs[:, :], idx_i[:, bass.ds(it * 4 + 2, 4)]).then_inc(M["idx_copied"], 1)
                pool.wait_ge(M["idx_copied"], it + 1)
                for u in range(4):
                    pool.wait_ge(M["zt4_done"], it * 8 + (2 * u + 2))
                    pool.sem_inc(M["gather_go"], 1)
                    gather(idxs[:, u:u + 1], zg_in[u % 2], ZG[u % 2])
            for n in range(NE - 2, NE):
                pool.wait_ge(M["zt4_done"], 2 * (n - 1))
                gather(idx_i[:, n:n + 1], zg_in[n % 2], ZG[n % 2])
            pool.wait_ge(zg_in[0], 16 * NE // 2)
            pool.wait_ge(zg_in[1], 16 * NE // 2)
            pool.wait_ge(M["zt4_done"], 2 * NE)
            total = pool.value_load(eid_i[0:1, OVER:OVER + 1], min_val=0, max_val=OVER)
            with pool.Fori(0, OVER) as n:
                with pool.If(total > n):
                    pool.tensor_copy(idxs[:, 0:1], idx_i[:, bass.ds(n + NE, 1)]).then_inc(M["over_idx"], 1)
                    pool.wait_ge(M["over_idx"], AFTER["over_idx"] + n + 1)
                    pool.sem_inc(M["gather_go"], 1)
                    gather(idxs[:, 0:1], zg_in[0], ZG[0])
                    pool.wait_ge(y_out[0], n * 16 + (8 * NE + 16))
            pool.wait_ge(y_out[0], 16 * NE // 2)
            pool.wait_ge(y_out[1], 16 * NE // 2)
            for s in range(NT):
                if s >= 2:
                    pool.wait_ge(M["co_ready"], s - 1)
                for c in range(2):
                    k = 2 * (s % 2) + c
                    col = slot_i[0:rows_of(s), c * NT + s:c * NT + s + 1]
                    pool.indirect_dma_start(out=CY[k][0:rows_of(s), :], out_offset=None, in_=y_d,
                                            in_offset=bass.IndirectOffsetOnAxis(ap=col, axis=0)).then_inc(cy_in[k], 16)

        @block.tensor
        def _(pe):
            pe.wait_ge(M["c_in"], 16)
            pe.wait_ge(M["small_in"], 16 * 16)
            pe.transpose(B[6][:, 0:NV], STAGE[0:NV, :], ident[0:NV, 0:NV])
            for c in range(CC):
                mm = pe.transpose(B[6][:, 64 + 32 * c:64 + 32 * c + TAPS], DWS[0:TAPS, c * 128:(c + 1) * 128], ident[0:TAPS, 0:TAPS])
            mm.then_inc(M["vec_tdone"], 1)

            def turn_z(n, rows):
                pe.wait_ge(M["z_ready"], n + 1)
                if n >= 1:
                    pe.wait_ge(M["ht_ready"], 2 * n)
                for half in range(2):
                    for c in range(4):
                        k = 4 * half + c
                        mm = pe.transpose(B[1 - half][:, c * 128:c * 128 + rows], Z[0:rows, k * 128:(k + 1) * 128], ident[0:rows, 0:rows])
                    mm.then_inc(M["zt_done"], 1)

            def project(bank, lo, hi, w, rows, at=0):
                for c in range(DC):
                    mm = pe.matmul(bank[0:rows, at:at + hi - lo], HT[:, c, 0:rows], w[:, c, lo:hi], start=(c == 0), stop=(c == DC - 1))
                return mm

            def ln_variance(s3):
                n3 = rows_of(s3)
                pe.wait_ge(M["ln_sq"], s3 + 1)
                for c in range(CC):
                    mm = pe.matmul(B[7][0:n3, 128:129], TMP[:, c * n3:(c + 1) * n3], meanw[:, 0:1], start=(c == 0), stop=(c == CC - 1))
                mm.then_inc(M["ln2_done"], 1)

            def ln_spread(s3):
                n3 = rows_of(s3)
                pe.wait_ge(M["ln_diag"], s3 + 1)
                pe.matmul(B[7][:, 256:256 + n3], meanw[0:n3, :], LND[0:n3, 0:n3], start=True, stop=True).then_inc(M["ln3_done"], 1)

            for m in range(2):
                turn_z(m, 128)
                pe.wait_ge(M["ht_ready"], 2 * m + 2)
                if m == 0:
                    pe.wait_ge(M["wmk_in"], 64)
                else:
                    pe.wait_ge(M["mk_normed"], 2)
                for half in range(2):
                    project(B[2 + half], 512 * half, 512 * half + 512, w_mk, 128).then_inc(M["mk_done"], 1)
                if m == 0:
                    pe.wait_ge(M["wmv_in"], 64)
                else:
                    pe.wait_ge(M["mv_ready"], 2)
                for half in range(2):
                    project(B[4 + half], 512 * half, 512 * half + 512, w_mv, 128).then_inc(M["mv_done"], 1)
                pe.wait_ge(M["mkn_ready"], m + 1)
                if m == 0:
                    pe.wait_ge(M["vec_ready"], 2)
                else:
                    pe.wait_ge(M["mktA_ready"], 1)
                    pe.wait_ge(M["mktD_ready"], 1)
                for half in range(2):
                    for c in range(4):
                        k = 4 * half + c
                        mm = pe.transpose(B[6 + half][:, c * 128:(c + 1) * 128], MK_N[:, k // 2, (k % 2) * 128:(k % 2) * 128 + 128], ident)
                    mm.then_inc(M["mkt_done"], 1)

            pe.wait_ge(M["mktA_ready"], 2)
            pe.wait_ge(M["mktD_ready"], 2)
            for it in range(NT + 2):
                s1, s2, s3 = it, it - 1, it - 2
                if s1 < NT:
                    n1 = rows_of(s1)
                    if s1 >= 2:
                        pe.wait_ge(M["ptA_ready"], 2 * (s1 - 1) - (1 if s1 >= 3 else 0))
                        pe.wait_ge(M["ptD_ready"], 2 * (s1 - 1) - (1 if s1 >= 3 else 0))
                    if s1 >= 3:
                        pe.wait_ge(M["x1_ready"], 2 * (s1 - 2))
                    turn_z(s1 + 2, n1)
                if 0 <= s2 < NT:
                    n2 = rows_of(s2)
                    pe.wait_ge(M["qn_ready"], s2 + 1)
                    if s2 == 0:
                        pe.wait_ge(M["skt_ready"], 2)
                    else:
                        pe.wait_ge(M["otA_ready"], s2)
                        pe.wait_ge(M["otD_ready"], s2)
                    for j in range(4):
                        mm = pe.transpose(B[6][:, j * 128:j * 128 + n2], QN[0:n2, j * 128:(j + 1) * 128], ident[0:n2, 0:n2])
                    mm.then_inc(M["qT_done"], 1)
                    pe.wait_ge(M["u_ready"], s2 + 1)
                    for c in range(CC):
                        mm = pe.transpose(B[7][:, c * 128:c * 128 + n2], U[0:n2, c * 128:(c + 1) * 128], ident[0:n2, 0:n2])
                    mm.then_inc(M["uT_done"], 1)
                    pe.wait_ge(M["kn_ready"], s2 + 1)
                    pe.wait_ge(M["v_ready"], s2 + 1)
                    pe.transpose(B[3][:, 256:256 + n2], KN[0:n2, :], ident[0:n2, 0:n2]).then_inc(M["kT_done"], 1)
                    pe.wait_ge(M["qT_ready"], s2 + 1)
                    pe.wait_ge(M["kT_ready"], s2 + 1)
                    if s2 == 0:
                        pe.wait_ge(M["qp_ready"], DEC_B)
                    for h in range(HEADS):
                        kv, j = h // 4, h % 4
                        part = slice(64 * kv, 64 * kv + 64)
                        out = B[2 + h // 2][0:n2, 256 * (h % 2):256 * (h % 2) + 256]
                        if s2 == 0:
                            for b in range(DEC_B):
                                pe.matmul(out[:, 0:128], QP[part, b, j, :], SKT[part, b, :], start=(b == 0), stop=(b == DEC_B - 1))
                            mm = pe.matmul(out[:, 128:192], QT[part, j, 0:n2], KT[0][part, 0:n2], start=True, stop=True)
                        else:
                            if s2 >= 2:
                                pe.matmul(out[:, 0:128], QT[part, j, :], KT[(s2 - 1) % 3][part, :], start=True, stop=True)
                            mm = pe.matmul(out[:, 128:256], QT[part, j, :], KT[s2 % 3][part, :], start=True, stop=True)
                        if h % 2 == 1:
                            mm.then_inc(M["sc_done"], 1)
                if 0 <= s3:
                    n3 = rows_of(s3)
                    pe.wait_ge(M["conv_tap"], CC * TAPS * (s3 + 1))
                    if 0 <= s2 < NT:
                        pe.wait_ge(M["uT_ready"], s2 + 1)
                    else:
                        pe.wait_ge(M["otD_ready"], NT)
                    for c in range(CC):
                        mm = pe.matmul(B[7][:, 0:n3], meanw, Y[s3][:, c, :], start=(c == 0), stop=(c == CC - 1))
                    mm.then_inc(M["ln1_done"], 1)
                if s1 < NT:
                    pe.wait_ge(M["ht_ready"], 2 * (s1 + 3))
                    if s1 == 0:
                        pe.wait_ge(M["win_in"], 64)
                    if s2 >= 0:
                        pe.wait_ge(M["s_ready"], 8 * s2 + 2)
                    project(B[2], 0, 512, w_in, n1).then_inc(M["pq_done"], 1)
                    if s2 >= 0:
                        pe.wait_ge(M["s_ready"], 8 * s2 + 4)
                    project(B[3], 512, 768, w_in, n1).then_inc(M["pkv_done"], 1)
                    if s3 >= 0:
                        ln_variance(s3)
                    if s2 >= 0:
                        pe.wait_ge(M["s_ready"], 8 * s2 + 6)
                    project(B[4], 1280, 1792, w_in, n1).then_inc(M["pub_done"], 1)
                    if s3 >= 0:
                        ln_spread(s3)
                    if s2 >= 0:
                        pe.wait_ge(M["s_ready"], 8 * s2 + 8)
                    project(B[5], 768, 1280, w_in, n1).then_inc(M["pua_done"], 1)
                    if s1 == 0:
                        pe.wait_ge(M["skv_in"], 80)
                        for half in range(2):
                            for b in range(4):
                                mm = pe.transpose(B[6 + half][:, b * 128:(b + 1) * 128], SK[:, 4 * half + b, :], ident)
                            mm.then_inc(M["skt_done"], 1)
                        for g in range(2):
                            for c in range(CC):
                                mm = pe.transpose(B[1 - g][:, c * 128:c * 128 + 4 * PAST], SST[0:4 * PAST, g, c * 128:(c + 1) * 128], ident[0:4 * PAST, 0:4 * PAST])
                            mm.then_inc(M["sst_done"], 1)
                        pe.wait_ge(M["sst_ready"], 2)
                elif s3 >= 0:
                    ln_variance(s3)
                    ln_spread(s3)
                if 0 <= s2 < NT:
                    pt = PTS if s2 == 0 else PT
                    kts = [1] if s2 == 1 else [0, 1]
                    seen = 0 if s2 == 0 else 2 * s2 - (1 if s2 >= 2 else 0)
                    pe.wait_ge(M["p_ready"], s2 + 1)
                    if s1 < NT:
                        pe.wait_ge(M["ht_ready"], 2 * (s1 + 3))
                    if s3 >= 1:
                        pe.wait_ge(M["x1_ready"], 2 * s3)
                    for k, kt in enumerate(kts):
                        keys = slice(kt * 128, kt * 128 + (n2 if s2 == 0 and kt else 128))
                        nk = keys.stop - keys.start
                        if k:
                            pe.wait_ge(M["ptA_ready"], seen + k)
                        for h in range(4):
                            mm = pe.transpose(B[0][0:nk, h * 128:h * 128 + n2], S[0:n2, h, keys], ident[0:n2, 0:n2])
                        mm.then_inc(M["ptA_done"], 1)
                        if k:
                            pe.wait_ge(M["ptD_ready"], seen + k)
                        for h in range(4):
                            mm = pe.transpose(B[1][0:nk, h * 128:h * 128 + n2], S[0:n2, 4 + h, keys], ident[0:n2, 0:n2])
                        mm.then_inc(M["ptD_done"], 1)
                if 0 <= s3:
                    if s3 == 0:
                        pe.wait_ge(M["wout_in"], 48)
                    pe.wait_ge(M["otA_ready"], s3 + 1)
                    pe.wait_ge(M["otD_ready"], s3 + 1)
                    pe.wait_ge(M["ct_ready"], s3 + 1)
                    if 0 <= s2 < NT:
                        pe.wait_ge(M["ptA_ready"], seen + len(kts))
                        pe.wait_ge(M["ptD_ready"], seen + len(kts))
                    elif s3 >= 1:
                        pe.wait_ge(M["x1_ready"], 2 * s3)
                    for half in range(2):
                        for c in range(8):
                            lhs = OT[:, c, 0:n3] if c < 4 else CT[:, c - 4, 0:n3]
                            mm = pe.matmul(B[half][0:n3, :], lhs, w_out[:, c, 512 * half:512 * half + 512], start=(c == 0), stop=(c == 7))
                        mm.then_inc(M["wo_done"], 1)
                if 0 <= s2 < NT:
                    if s3 >= 0:
                        pe.wait_ge(M["lnr_ready"], s3 + 1)
                    for half, (got, done) in enumerate((("ptA_ready", "pvA_done"), ("ptD_ready", "pvD_done"))):
                        pe.wait_ge(M[got], seen + len(kts))
                        heads = slice(4 * half, 4 * half + 4)
                        if s2 == 0:
                            out = B[6 + half][:, 0:4 * n2].rearrange("p (h t) -> p h t", h=4)
                            mm = pe.matmul(out, VV[0][0:n2, :], pt[0:n2, 1, heads, :], start=True, stop=False, skip_group_check=True)
                            for b in range(DEC_B):
                                cols = slice(b * DEC_T, (b + 1) * DEC_T)
                                mm = pe.matmul(out[:, :, cols], SV[:, b, :], pt[:, 0, heads, cols], start=False, stop=(b == DEC_B - 1), skip_group_check=True)
                        else:
                            for k, kt in enumerate(kts):
                                mm = pe.matmul(B[6 + half][:, :], VV[(s2 - 1 + kt) % 3], pt[:, kt, heads, :], start=(k == 0), stop=(k == len(kts) - 1))
                        mm.then_inc(M[done], 1)

            pe.wait_ge(M["x1_ready"], 2 * NT)
            for it in range(NT + 2):
                s1, s2, s3 = it, it - 1, it - 2
                if s1 < NT:
                    n1 = rows_of(s1)
                    if s1 >= 2:
                        pe.wait_ge(M["pt2A_ready"], AFTER["pt2A_ready"] + s1 - 1)
                        pe.wait_ge(M["pt2D_ready"], AFTER["pt2D_ready"] + s1 - 1)
                    if s1 >= 3:
                        pe.wait_ge(M["h3_ready"], 2 * (s1 - 2))
                    turn_z(s1 + NT + 2, n1)
                if 0 <= s2 < NT:
                    n2 = rows_of(s2)
                    pe.wait_ge(M["q2n_ready"], AFTER["q2n_ready"] + 2 * s2 + 2)
                    if s2 >= 1:
                        pe.wait_ge(M["ot2A_ready"], AFTER["ot2A_ready"] + s2)
                        pe.wait_ge(M["ot2D_ready"], AFTER["ot2D_ready"] + s2)
                    for half in range(2):
                        for c in range(4):
                            k = 4 * half + c
                            mm = pe.transpose(B[6 + half][:, c * 128:c * 128 + n2], QN2[0:n2, k // 2, (k % 2) * 128:(k % 2) * 128 + 128], ident[0:n2, 0:n2])
                        mm.then_inc(M["q2T_done"], 1)
                    pe.wait_ge(M["q2T_ready"], AFTER["q2T_ready"] + 2 * s2 + 2)
                    if s2 >= 1:
                        pe.wait_ge(M["x2_ready"], AFTER["x2_ready"] + 2 * s2)
                    if s2 == 0:
                        pe.wait_ge(M["qp2_ready"], AFTER["qp2_ready"] + DEC_B)
                        for b in range(DEC_B):
                            pe.wait_ge(mk_in[b % 2], 16 * (b // 2 + 1))
                            for mt in range(2):
                                for half, (got, done) in enumerate((("mkbA_ready", "mkb_tA"), ("mkbD_ready", "mkb_tD"))):
                                    if 2 * b + mt:
                                        pe.wait_ge(M[got], AFTER[got] + 2 * b + mt)
                                    for c in range(4):
                                        k = 4 * half + c
                                        mm = pe.transpose(B[4 + half][:, c * 128:(c + 1) * 128], MKB[b % 2][:, mt, k * 128:(k + 1) * 128], ident)
                                    mm.then_inc(M[done], 1)
                            pe.wait_ge(M["mkbA_ready"], AFTER["mkbA_ready"] + 2 * b + 2)
                            pe.wait_ge(M["mkbD_ready"], AFTER["mkbD_ready"] + 2 * b + 2)
                            for c in range(DC):
                                h = c // 2
                                mm = pe.matmul(B[2 + h // 2][0:n2, 256 * (h % 2):256 * (h % 2) + 256], QP2[:, b, c, :], MKTB[:, c, :],
                                               start=(b == 0 and c % 4 == 0), stop=(b == DEC_B - 1 and c % 4 == 3), skip_group_check=True)
                            mm.then_inc(M["mkb_used"], 1)
                        mm = None
                    else:
                        for h in range(MH):
                            for dc in range(2):
                                mm = pe.matmul(B[2 + h // 2][0:n2, 256 * (h % 2):256 * (h % 2) + 256], QT2[:, 2 * h + dc, :], MKT[:, 2 * h + dc, :], start=(dc == 0), stop=(dc == 1))
                            if h % 2 == 1:
                                mm.then_inc(M["sc2_done"], 1)
                if s1 < NT:
                    pe.wait_ge(M["ht_ready"], 2 * (s1 + NT + 3))
                    if s1 == 0:
                        pe.wait_ge(M["wmq_in"], 64)
                    if s1 == 1:
                        pe.wait_ge(M["mkbA_ready"], AFTER["mkbA_ready"] + 2 * DEC_B)
                        pe.wait_ge(M["mkbD_ready"], AFTER["mkbD_ready"] + 2 * DEC_B)
                    for half in range(2):
                        project(B[4 + half], 512 * half, 512 * half + 512, w_mq, n1).then_inc(M["mq_done"], 1)
                if 0 <= s2 < NT:
                    pe.wait_ge(M["p2_ready"], AFTER["p2_ready"] + s2 + 1)
                    if s1 >= 3:
                        pe.wait_ge(M["h3_ready"], 2 * (s1 - 2))
                    for mt in range(2):
                        for h in range(MH):
                            mm = pe.transpose(B[mt][:, h * 128:h * 128 + n2], S2[0:n2, h, mt * 128:(mt + 1) * 128], ident[0:n2, 0:n2])
                        mm.then_inc(M["pt2A_done" if mt == 0 else "pt2D_done"], 1)
                    pe.wait_ge(M["pt2A_ready"], AFTER["pt2A_ready"] + s2 + 1)
                    pe.wait_ge(M["pt2D_ready"], AFTER["pt2D_ready"] + s2 + 1)
                    if s2 == 0:
                        for b in range(DEC_B):
                            pe.wait_ge(mv_in[b % 2], 16 * (b // 2 + 1))
                            cols = slice(b * DEC_T, (b + 1) * DEC_T)
                            for c in range(DC):
                                for mt in range(2):
                                    mm = pe.matmul(B[6 + c // 4][:, (c % 4) * 128 + b * DEC_T:(c % 4) * 128 + (b + 1) * DEC_T],
                                                   MVB[b % 2][:, mt, c * 128:(c + 1) * 128], PT2[:, mt, c // 2, cols], start=(mt == 0), stop=(mt == 1))
                            mm.then_inc(M["mvb_used"], 1)
                    else:
                        for c in range(DC):
                            for mt in range(2):
                                mm = pe.matmul(B[6 + c // 4][:, (c % 4) * 128:(c % 4) * 128 + 128], MV[:, mt, c * 128:(c + 1) * 128], PT2[:, mt, c // 2, :], start=(mt == 0), stop=(mt == 1))
                            if c % 4 == 3:
                                mm.then_inc(M["pv2A_done" if c == 3 else "pv2D_done"], 1)
                if 0 <= s3:
                    n3 = rows_of(s3)
                    pe.wait_ge(M["z3_ready"], s3 + 1)
                    for half in range(2):
                        for c in range(4):
                            k = 4 * half + c
                            mm = pe.transpose(B[half][:, c * 128:c * 128 + n3], Z3[0:n3, k * 128:(k + 1) * 128], ident[0:n3, 0:n3])
                        mm.then_inc(M["z3t_done"], 1)
                    pe.wait_ge(M["h3_ready"], 2 * s3 + 2)
                    pe.wait_ge(M["wr_in"], 32)
                    wr = view(WR, 0, DC, 36)
                    for c in range(DC):
                        mm = pe.matmul(B[2][0:n3, 0:36], H3[:, c, 0:n3], wr[:, c, :], start=(c == 0), stop=(c == DC - 1))
                    mm.then_inc(M["rt_done"], 1)
                if 0 <= s2 < NT:
                    if s2 == 0:
                        pe.wait_ge(M["wmo_in"], 64)
                    pe.wait_ge(M["ot2A_ready"], AFTER["ot2A_ready"] + s2 + 1)
                    pe.wait_ge(M["ot2D_ready"], AFTER["ot2D_ready"] + s2 + 1)
                    for half in (1, 0):
                        if half == 0 and s3 >= 0:
                            pe.wait_ge(M["lg_ready"], s3 + 1)
                        for c in range(DC):
                            mm = pe.matmul(B[2 + half][0:n2, :], OT2[:, c, 0:n2], w_mo[:, c, 512 * half:512 * half + 512], start=(c == 0), stop=(c == DC - 1))
                        mm.then_inc(M["mo_done"], 1)

            pe.wait_ge(M["r_mask"], AFTER["r_mask"] + 1)
            pe.wait_ge(M["lg_ready"], NT)
            pe.wait_ge(M["rconst_in"], 16)
            pe.matmul(B[0][:, 0:288], tri, RM, start=True, stop=False)
            pe.matmul(B[0][:, 0:288], ones, RA, start=False, stop=True)
            pe.matmul(B[1][0:32, 0:1], RTOT, ones[:, 0:1], start=True, stop=True).then_inc(M["r_pref"], 1)
            pe.wait_ge(M["r_ov"], AFTER["r_ov"] + 1)
            pe.matmul(B[1][:, 64:97], ROV[0:32, :], tri33[0:32, :], start=True, stop=True).then_inc(M["r_base"], 1)
            pe.wait_ge(M["r_rows"], AFTER["r_rows"] + 1)
            for k in range(2 * NT):
                mm = pe.matmul(B[2][:, 0:NSLOT], RR[:, k, :], RQ[:, k, :], start=(k == 0), stop=(k == 2 * NT - 1))
            mm.then_inc(M["r_table"], 1)

            def turn_rows(n, u, rows_in, count, banks=(0, 1)):
                pe.wait_ge(rows_in, count)
                for half in range(2):
                    for c in range(4):
                        k = 4 * half + c
                        mm = pe.transpose(B[half][:, c * 128:(c + 1) * 128], ZG[u][:, k * 128:(k + 1) * 128], ident)
                    yield mm

            def gate_up(u, par):
                for c in range(DC):
                    mm = pe.matmul(B[2 + par][:, :], HG[par][:, c, :], WGU[u][:, c, :], start=(c == 0), stop=(c == DC - 1))
                return mm

            def down(u, par):
                for half in range(2):
                    for c in range(2):
                        mm = pe.matmul(B[6 + half][:, :], AT[par][:, c, :], WD[u][:, c, 512 * half:512 * half + 512], start=(c == 0), stop=(c == 1))
                    yield mm

            def expert_step(n, u, more1, more2, first=False):
                p = u % 2
                if more1:
                    pe.wait_ge(M["hg_ready"], n * 2 + 4)
                    pe.wait_ge(wexp_in[(u + 1) % 4], ((n + 1) // 4 + 1) * 48 if isinstance(n, int) else (n - u + (4 if u == 3 else 0)) * 12 + 48)
                    if not first:
                        pe.wait_ge(M["ab_ready"], n)
                    gate_up((u + 1) % 4, 1 - p).then_inc(M["gu_done"], 1)
                if more2:
                    for mm in turn_rows(n, p, zg_in[p], (n // 2 + 2) * 16 if isinstance(n, int) else (n - u) * 8 + (u // 2 + 2) * 16):
                        mm.then_inc(M["zt4_done"], 1)
                pe.wait_ge(M["ab_ready"], n + 1)
                for c in range(2):
                    mm = pe.transpose(B[4 + p][:, c * 128:(c + 1) * 128], AB[p][:, c * 128:(c + 1) * 128], ident)
                mm.then_inc(M["at_done"], 1)
                pe.wait_ge(M["at_ready"], n + 1)
                if not first:
                    pe.wait_ge(M["yb_readyA"], n)
                    pe.wait_ge(M["yb_readyD"], n)
                for mm in down(u, p):
                    mm.then_inc(M["dn_done"], 1)

            pe.wait_ge(M["route_ready"], 1)
            for mm in turn_rows(0, 0, zg_in[0], 16):
                mm.then_inc(M["zt4_done"], 1)
            pe.wait_ge(M["hg_ready"], 2)
            pe.wait_ge(wexp_in[0], 48)
            gate_up(0, 0).then_inc(M["gu_done"], 1)
            for mm in turn_rows(1, 1, zg_in[1], 16):
                mm.then_inc(M["zt4_done"], 1)
            for u in range(4):
                expert_step(u, u, True, True, first=(u == 0))
            with pe.Fori(1, NE // 4 - 1) as it:
                for u in range(4):
                    expert_step(it * 4 + u, u, True, True)
            for u in range(4):
                n = NE - 4 + u
                expert_step(n, u, n + 1 < NE, n + 2 < NE)
            pe.wait_ge(M["yb_readyA"], NE)
            pe.wait_ge(M["yb_readyD"], NE)
            total = pe.value_load(eid_i[0:1, OVER:OVER + 1], min_val=0, max_val=OVER)
            with pe.Fori(0, OVER) as n:
                with pe.If(total > n):
                    for mm in turn_rows(0, 0, zg_in[0], n * 16 + (8 * NE + 16)):
                        mm.then_inc(M["over_t"], 1)
                    pe.wait_ge(M["over_h"], AFTER["over_h"] + n * 2 + 2)
                    pe.wait_ge(wexp_in[0], n * 48 + (12 * NE + 48))
                    gate_up(0, 0).then_inc(M["over_gu"], 1)
                    pe.wait_ge(M["ab_ready"], n + (NE + 1))
                    for c in range(2):
                        mm = pe.transpose(B[4][:, c * 128:(c + 1) * 128], AB[0][:, c * 128:(c + 1) * 128], ident)
                    mm.then_inc(M["over_at"], 1)
                    pe.wait_ge(M["over_atr"], AFTER["over_atr"] + n + 1)
                    for mm in down(0, 0):
                        mm.then_inc(M["over_dn"], 1)
                    pe.wait_ge(M["over_yA"], AFTER["over_yA"] + n + 1)
                    pe.wait_ge(M["over_yD"], AFTER["over_yD"] + n + 1)

        @block.scalar
        def _(act):
            act.wait_ge(M["vec_tdone"], 1)
            act.activation(cvec[:, 0:NV], B[6][:, 0:NV], ACT.Copy).then_inc(M["vec_ready"], 1)
            act.activation(view(dwT, 0, CC, TAPS), B[6][:, 64:192].rearrange("p (c t) -> p c t", c=CC)[:, :, 0:TAPS], ACT.Copy).then_inc(M["vec_ready"], 1)

            def sum_sq(n, rows, src):
                act.activation(JUNK[0:rows, :], src[0:rows, :], ACT.Square, accum_out=st[0:rows, n % 2:n % 2 + 1]).then_inc(M["x_sq"], 1)

            act.wait_ge(x_in[0], 16)
            sum_sq(0, 128, XR[0])
            for m in range(2):
                for half in range(2):
                    act.wait_ge(M["mk_done"], 2 * m + half + 1)
                    if half == 0:
                        act.wait_ge(M["zt_done"], 2 * m + 2)
                    act.activation(Z[:, 512 * half:512 * half + 512], B[2 + half][:, :], ACT.Square).then_inc(M["mk_sq"], 1)
                act.wait_ge(x_in[m + 1], 16)
                act.wait_ge(M["x_sq"], m + 1)
                sum_sq(m + 1, 128 if m == 0 else rows_of(0), XR[m + 1])
                for half in range(2):
                    act.wait_ge(M["mv_done"], 2 * m + half + 1)
                    act.activation(MV[:, m, 512 * half:512 * half + 512], B[4 + half][:, :], ACT.Copy).then_inc(M["mv_ready"], 1)
                act.wait_ge(M["mkt_done"], 2 * m + 1)
                act.activation(MKT[:, 0:4, m * 128:(m + 1) * 128], B[6][:, :].rearrange("p (c t) -> p c t", c=4), ACT.Copy).then_inc(M["mktA_ready"], 1)
                act.wait_ge(M["mkn_ready"], m + 1)
                act.dma_start(o["mem_k"][0, 0, m * 128:(m + 1) * 128].rearrange("t h d -> t (h d)"), MK_N.rearrange("p h d -> p (h d)")).then_inc(M["mem_out"], 16)
                act.wait_ge(M["mv_ready"], 2 * m + 2)
                act.dma_start(o["mem_v"][0, 0, m * 128:(m + 1) * 128].rearrange("t h d -> t (h d)"), MV[:, m, :]).then_inc(M["mem_out"], 16)
            for it in range(NT + 2):
                s1, s2, s3 = it, it - 1, it - 2
                if 0 <= s2 < NT:
                    n2 = rows_of(s2)
                    act.wait_ge(M["qT_done"], s2 + 1)
                    if s2 == 0:
                        act.wait_ge(M["vec_ready"], 2)
                    act.activation(QT[:, :, 0:n2], B[6][:, :].rearrange("p (j t) -> p j t", j=4)[:, :, 0:n2], ACT.Copy, scale=cvec[:, V_GQ:V_GQ + 1]).then_inc(M["qT_ready"], 1)
                    act.wait_ge(M["uT_done"], s2 + 1)
                    src = B[7][:, :].rearrange("p (c t) -> p c t", c=CC)
                    if s2 == 0:
                        act.activation(UTS[:, :, :, PAST:PAST + DEC_T], src[:, :, 0:n2].rearrange("p c (b t) -> p c b t", t=DEC_T), ACT.Copy).then_inc(M["uT_ready"], 1)
                    else:
                        act.wait_ge(M["conv_tap"], CC * TAPS * max(s2 - 1, 1))
                        act.wait_ge(M["halo"], s2)
                        act.activation(UT[s2 % 2][:, :, PAST:PAST + 128], src, ACT.Copy).then_inc(M["uT_ready"], 1)
                    act.wait_ge(M["nm_ready"], s2 + 1)
                    c0, c1 = key_range(s2)
                    for h in range(HEADS):
                        act.activation(S[0:n2, h, c0:c1], S[0:n2, h, c0:c1], ACT.Exp, bias=st[0:n2, 50 + h:51 + h], scale=SCALE,
                                       accum_out=st[0:n2, 58 + h:59 + h]).then_inc(M["s_exp"], 1)
                    act.activation(st[0:n2, 74:82], st[0:n2, 66:74], ACT.Exp).then_inc(M["s_exp"], 1)
                if 0 <= s3:
                    n3 = rows_of(s3)
                    act.wait_ge(M["xc_ready"], s3 + 1)
                    act.activation(TMP[:, 0:CC * n3], Y[s3].rearrange("p c t -> p (c t)"), ACT.Square).then_inc(M["ln_sq"], 1)
                    act.wait_ge(M["v_act"], CC * (s3 + 1))
                    act.wait_ge(M["ln2_done"], s3 + 1)
                    act.activation(TMP[:, 0:CC * n3], Y[s3].rearrange("p c t -> p (c t)"), ACT.Exp, scale=-1.0).then_inc(M["ln_exp"], 1)
                if s1 < NT:
                    n1 = rows_of(s1)
                    act.wait_ge(M["pub_done"], s1 + 1)
                    if s1 >= 1:
                        act.wait_ge(M["uT_done"], s1)
                    if s1 == 1:
                        act.wait_ge(M["kvu_out"], 16 * 3 * DEC_B)
                    act.activation(U[0:n1, :], B[4][0:n1, :], ACT.Exp, scale=-1.0).then_inc(M["ub_exp"], 1)
                    if s1 == 0:
                        for half in range(2):
                            act.wait_ge(M["skt_done"], half + 1)
                            act.activation(SKT[:, 4 * half:4 * half + 4, :], B[6 + half][:, :].rearrange("p (b t) -> p b t", b=4), ACT.Copy).then_inc(M["skt_ready"], 1)
                        act.wait_ge(M["mktA_ready"], 2)
                        act.wait_ge(M["mktD_ready"], 2)
                        for g in range(2):
                            act.wait_ge(M["sst_done"], g + 1)
                            for b in range(4):
                                a = act.activation(UTS[:, :, 4 * g + b, 0:PAST],
                                                   B[1 - g][:, :].rearrange("p (c t) -> p c t", c=CC)[:, :, PAST * b:PAST * b + PAST], ACT.Copy)
                            a.then_inc(M["sst_ready"], 1)
                if 0 <= s2 < NT:
                    pt = PTS if s2 == 0 else PT
                    kts = [1] if s2 == 1 else [0, 1]
                    seen = 0 if s2 == 0 else 2 * s2 - (1 if s2 >= 2 else 0)
                    for k, kt in enumerate(kts):
                        nk = n2 if s2 == 0 and kt else 128
                        act.wait_ge(M["ptA_done"], seen + k + 1)
                        if k == 0 and s2 >= 1:
                            act.wait_ge(M["pvD_done"], s2)
                        act.activation(pt[0:nk, kt, 0:4, :], B[0][0:nk, :].rearrange("p (h t) -> p h t", h=4)[:, :, 0:n2], ACT.Copy).then_inc(M["ptA_ready"], 1)
                if s1 < NT:
                    act.wait_ge(M["pq_done"], s1 + 1)
                    act.wait_ge(M["zt_done"], 2 * (s1 + 3))
                    act.activation(Z[0:n1, 0:512], B[2][0:n1, :], ACT.Square).then_inc(M["qk_sq"], 1)
                    act.wait_ge(M["pkv_done"], AFTER["pkv_done"] + s1 + 1)
                    if s1 >= 1:
                        act.wait_ge(M["kT_done"], s1)
                    act.activation(KN[0:n1, :], B[3][0:n1, 0:128], ACT.Square).then_inc(M["qk_sq"], 1)
                if s1 < NT:
                    nxt = s1 + 1
                    if s2 >= 0:
                        act.wait_ge(M["ptD_done"], seen + len(kts))
                    if nxt < NT:
                        act.wait_ge(x_in[(nxt + 2) % 4], 16 * ((nxt + 2) // 4 + 1))
                        src = XR[(nxt + 2) % 4]
                        sum_sq(nxt + 2, rows_of(nxt), src)
                if 0 <= s2 < NT:
                    act.wait_ge(M["pvA_done"], s2 + 1)
                    src = B[6][0:64, 0:4 * n2].rearrange("p (j t) -> p j t", j=4)
                    if s2 >= 1:
                        act.wait_ge(M["wo_done"], 2 * s2)
                    act.activation(OT[0:64, :, 0:n2], src, ACT.Copy).then_inc(M["otA_ready"], 1)
                if it == NT + 1:
                    act.wait_ge(x1_in[0], 16)
                    act.wait_ge(M["ptD_done"], 2 * NT - 1)
                    sum_sq(NT + 2, rows_of(0), XR[0])

            for it in range(NT + 2):
                s1, s2, s3 = it, it - 1, it - 2
                if 0 <= s3:
                    n3 = rows_of(s3)
                    act.wait_ge(M["x2_ready"], AFTER["x2_ready"] + 2 * s3 + 2)
                    act.activation(SQ2[0:n3, :], XR[s3 % 4][0:n3, :], ACT.Square, accum_out=st[0:n3, 40:41]).then_inc(M["z3_sq"], 1)
                if s2 == 0:
                    for b in range(DEC_B):
                        for mt in range(2):
                            act.wait_ge(M["mkb_tA"], AFTER["mkb_tA"] + 2 * b + mt + 1)
                            if b:
                                act.wait_ge(M["mkb_used"], b)
                            act.activation(MKTB[:, 0:4, mt * 128:(mt + 1) * 128], B[4][:, :].rearrange("p (c t) -> p c t", c=4), ACT.Copy).then_inc(M["mkbA_ready"], 1)
                if 0 <= s2 < NT:
                    n2 = rows_of(s2)
                    act.wait_ge(M["nm2_ready"], AFTER["nm2_ready"] + s2 + 1)
                    if s2 >= 1:
                        act.wait_ge(M["pt2D_done"], AFTER["pt2D_done"] + s2)
                    for h in range(MH):
                        act.activation(S2[0:n2, h, :], B[2 + h // 2][0:n2, 256 * (h % 2):256 * (h % 2) + 256], ACT.Exp, bias=st[0:n2, 50 + h:51 + h], scale=MSCALE,
                                       accum_out=st[0:n2, 58 + h:59 + h]).then_inc(M["s2_exp"], 1)
                    act.wait_ge(M["pt2A_done"], AFTER["pt2A_done"] + s2 + 1)
                    if s2 >= 1:
                        act.wait_ge(M["pv2D_done"], AFTER["pv2D_done"] + s2 - 1) if s2 >= 2 else act.wait_ge(M["mvb_used"], DEC_B)
                    act.activation(PT2[:, 0, :, 0:n2], B[0][:, :].rearrange("p (h t) -> p h t", h=4)[:, :, 0:n2], ACT.Copy).then_inc(M["pt2A_ready"], 1)
                    if s2 == 0:
                        act.wait_ge(M["mvb_used"], DEC_B)
                    else:
                        act.wait_ge(M["pv2A_done"], AFTER["pv2A_done"] + s2)
                        act.wait_ge(M["mo_done"], AFTER["mo_done"] + 2 * s2)
                    act.activation(OT2[:, 0:4, 0:n2], B[6][:, :].rearrange("p (c t) -> p c t", c=4)[:, :, 0:n2], ACT.Copy).then_inc(M["ot2A_ready"], 1)
                if s1 < NT:
                    n1 = rows_of(s1)
                    act.wait_ge(M["zt_done"], 2 * (s1 + NT + 3))
                    for half in range(2):
                        act.wait_ge(M["mq_done"], AFTER["mq_done"] + 2 * s1 + half + 1)
                        act.activation(Z[0:n1, 512 * half:512 * half + 512], B[4 + half][0:n1, :], ACT.Square).then_inc(M["q2_sq"], 1)
                if s1 + 1 < NT:
                    nxt = s1 + 1
                    act.wait_ge(x1_in[nxt % 4], 16 * (nxt // 4 + 1))
                    if s3 >= 0:
                        act.wait_ge(M["z3_sq"], s3 + 1)
                    act.wait_ge(M["x_sq"], nxt + NT + 2)
                    act.activation(SQ3[0:rows_of(nxt), :], XR[nxt % 4][0:rows_of(nxt), :], ACT.Square,
                                   accum_out=st[0:rows_of(nxt), (nxt + NT + 2) % 2:(nxt + NT + 2) % 2 + 1]).then_inc(M["x_sq"], 1)

            act.wait_ge(M["r_arg"], 1)
            act.activation(R_EG, R_EG, ACT.Exp).then_inc(M["r_exp"], 1)
            act.wait_ge(M["r_arg"], 2)
            act.activation(R_E2, R_E2, ACT.Exp).then_inc(M["r_exp"], 1)

            def expert_step(n, u, first):
                p = u % 2
                act.wait_ge(M["gu_done"], n + 1)
                act.activation(EB[p], B[2 + p][:, 0:FE], ACT.Exp, scale=-1.0).then_inc(M["gu_exp"], 1)
                act.wait_ge(M["at_done"], n + 1)
                act.activation(AT[p], B[4 + p][:, 0:256].rearrange("p (c t) -> p c t", c=2), ACT.Copy).then_inc(M["at_ready"], 1)
                if not first:
                    act.wait_ge(y_out[p], (n // 2) * 16 if isinstance(n, int) else (n - u) * 8 + (u // 2) * 16)
                act.wait_ge(M["dn_done"], n * 2 + 1)
                act.activation(YB[p][:, 0:512], B[6][:, :], ACT.Copy).then_inc(M["yb_readyA"], 1)
            for u in range(4):
                expert_step(u, u, u < 2)
            with act.Fori(1, NE // 4) as it:
                for u in range(4):
                    expert_step(it * 4 + u, u, False)
            act.wait_ge(y_out[0], 16 * NE // 2)
            total = act.value_load(eid_i[0:1, OVER:OVER + 1], min_val=0, max_val=OVER)
            with act.Fori(0, OVER) as n:
                with act.If(total > n):
                    act.wait_ge(M["over_gu"], AFTER["over_gu"] + n + 1)
                    act.activation(EB[0], B[2][:, 0:FE], ACT.Exp, scale=-1.0).then_inc(M["over_e"], 1)
                    act.wait_ge(M["over_at"], AFTER["over_at"] + n + 1)
                    act.activation(AT[0], B[4][:, 0:256].rearrange("p (c t) -> p c t", c=2), ACT.Copy).then_inc(M["over_atr"], 1)
                    act.wait_ge(y_out[0], n * 16 + 8 * NE)
                    act.wait_ge(M["over_dn"], AFTER["over_dn"] + n * 2 + 1)
                    act.activation(YB[0][:, 0:512], B[6][:, :], ACT.Copy).then_inc(M["over_yA"], 1)

        @block.vector
        def _(dve):
            steps = [0]

            def link(ins):
                steps[0] += 1
                ins.then_inc(M["dve"], 1)
                dve.wait_ge(M["dve"], steps[0])

            def gain(v, n, rows=128):
                return cvec[:, v:v + n][:, :, None].to_broadcast([128, n, rows])

            def norm_z(n, rows, src):
                dve.wait_ge(M["x_rs"], n + 1)
                if n >= 1:
                    dve.wait_ge(M["zt_done"], 2 * n)
                dve.tensor_scalar(Z[0:rows, :], src[0:rows, :], st[0:rows, 2 + n % 2:3 + n % 2], None, ALU.mult).then_inc(M["z_ready"], 1)

            def take_hT(n, rows, v):
                for half in range(2):
                    dve.wait_ge(M["zt_done"], 2 * n + half + 1)
                    src = B[1 - half][:, :].rearrange("p (c t) -> p c t", c=4)[:, :, 0:rows]
                    dve.tensor_tensor(HT[:, 4 * half:4 * half + 4, 0:rows], src, gain(v + 4 * half, 4, rows), ALU.mult).then_inc(M["ht_ready"], 1)

            link(dve.memset(LG[:, :], 0.0))
            dve.wait_ge(M["small_in"], 16 * 16)
            dve.tensor_scalar(sink8[:, :], sink_bc[:, :], 1.0 / SCALE, None, ALU.mult).then_inc(M["dve"], 1)
            steps[0] += 1
            dve.wait_ge(x_in[0], 16)
            norm_z(0, 128, XR[0])
            for m in range(2):
                dve.wait_ge(M["vec_ready"], 2)
                if m:
                    dve.wait_ge(M["mv_done"], 2)
                take_hT(m, 128, V_MEM)
                dve.wait_ge(M["mk_sq"], 2 * m + 2)
                if m:
                    dve.wait_ge(M["mk_rs"], 1)
                dve.tensor_reduce(st[:, 4:8], Z.rearrange("p (h d) -> p h d", h=MH), X, ALU.add).then_inc(M["mk_ssq"], 1)
                dve.wait_ge(M["mk_ssq"], m + 1)
                if m == 0:
                    norm_z(1, 128, XR[1])
                else:
                    norm_z(2, rows_of(0), XR[2])
                dve.wait_ge(M["mk_rs"], m + 1)
                if m:
                    dve.wait_ge(M["mkt_done"], 2)
                    dve.wait_ge(M["mem_out"], 32)
                for half in range(2):
                    dve.tensor_tensor(MK_N[:, 2 * half:2 * half + 2, :], B[2 + half][:, :].rearrange("p (h d) -> p h d", h=2),
                                      bc(st[:, 8 + 2 * half:10 + 2 * half], MHD, 2), ALU.mult).then_inc(M["mk_normed"], 1)
                dve.wait_ge(M["mk_normed"], 2 * m + 2)
                dve.tensor_tensor(MK_N, MK_N, bc(GMK, MH, 1), ALU.mult).then_inc(M["mkn_ready"], 1)
                dve.wait_ge(M["mkt_done"], 2 * m + 2)
                dve.tensor_copy(MKT[:, 4:8, m * 128:(m + 1) * 128], B[7][:, :].rearrange("p (c t) -> p c t", c=4)).then_inc(M["mktD_ready"], 1)

            def conv_taps(s, k0, k1):
                n = rows_of(s)
                base = CC * TAPS * s
                for k in range(k0, k1):
                    tap, c = k // CC, k % CC
                    w = dwT[:, c * TAPS + tap:c * TAPS + tap + 1]
                    if s == 0:
                        src = UTS[:, c, :, tap:tap + DEC_T]
                        y = Y[s][:, c, :].rearrange("p (b t) -> p b t", t=DEC_T)
                    else:
                        src = UT[s % 2][:, c, tap:tap + 128]
                        y = Y[s][:, c, :]
                    if tap == 0:
                        dve.tensor_scalar(y, src, w, cvec[:, V_DWB + c:V_DWB + c + 1], ALU.mult, ALU.add).then_inc(M["conv_tap"], 1)
                    else:
                        dve.wait_ge(M["conv_tap"], base + k - CC + 1)
                        dve.scalar_tensor_tensor(y, src, w, y, ALU.mult, ALU.add).then_inc(M["conv_tap"], 1)

            CUTS = [28, 44, 52, 64, 72]
            for it in range(NT + 2):
                s1, s2, s3 = it, it - 1, it - 2
                if s1 < NT:
                    n1 = rows_of(s1)
                    if s1 >= 1:
                        dve.wait_ge(M["pua_done"], AFTER["pua_done"] + s1)
                    else:
                        dve.wait_ge(M["mv_done"], 4)
                    take_hT(s1 + 2, n1, V_MIX)
                if 0 <= s2 < NT:
                    n2 = rows_of(s2)
                    c0, c1 = key_range(s2)
                    dve.wait_ge(M["kT_done"], s2 + 1)
                    if s2 >= 2:
                        dve.wait_ge(M["sc_done"], 4 * (s2 - 1))
                    dve.tensor_copy(KT[s2 % 3][:, 0:n2], B[3][:, 256:256 + n2]).then_inc(M["kT_ready"], 1)
                    if s2 == 0:
                        dve.wait_ge(M["qT_ready"], 1)
                        dve.wait_ge(M["qp_zero"], 1)
                        for b in range(DEC_B):
                            cols = slice(b * DEC_T, (b + 1) * DEC_T)
                            dve.tensor_copy(QP[:, b, :, cols], QT[:, :, cols]).then_inc(M["qp_ready"], 1)
                        dve.wait_ge(M["skv_in"], 80)
                        dve.wait_ge(M["mem_out"], 64)
                    if s2 == 1:
                        dve.wait_ge(M["dist_in"], 16)
                    dist = DIST_S if s2 == 0 else DIST
                    dve.wait_ge(M["x_sq"], min(s2 + 4, NT + 2))
                    for h in range(HEADS):
                        if h % 2 == 0:
                            dve.wait_ge(M["sc_done"], 4 * s2 + h // 2 + 1)
                        dve.scalar_tensor_tensor(S[0:n2, h, c0:c1], dist[0:n2, c0:c1], -(2.0 ** -(h + 1)) / SCALE,
                                                 B[2 + h // 2][0:n2, 256 * (h % 2) + c0:256 * (h % 2) + c1], ALU.mult, ALU.add).then_inc(M["s_ready"], 1)
                    dve.wait_ge(M["s_ready"], 8 * s2 + 8)
                    link(dve.tensor_reduce(st[0:n2, 42:50], S[0:n2, :, c0:c1], X, ALU.max))
                    link(dve.tensor_tensor(st[0:n2, 42:50], st[0:n2, 42:50], sink8[0:n2, :], ALU.max))
                    if s2:
                        dve.wait_ge(M["s_exp"], 9 * s2)
                    link(dve.tensor_scalar(st[0:n2, 50:58], st[0:n2, 42:50], -SCALE, None, ALU.mult))
                    dve.tensor_tensor(st[0:n2, 66:74], st[0:n2, 50:58], sink_bc[0:n2, :], ALU.add).then_inc(M["nm_ready"], 1)
                if 0 <= s3:
                    n3 = rows_of(s3)
                    dve.wait_ge(M["ln1_done"], s3 + 1)
                    dve.tensor_tensor(Y[s3], Y[s3], bc(B[7][:, 0:n3], CC, 1), ALU.subtract).then_inc(M["xc_ready"], 1)
                if 0 <= s2 < NT:
                    if s2 == 0:
                        dve.wait_ge(M["sst_ready"], 2)
                    dve.wait_ge(M["uT_ready"], s2 + 1)
                    conv_taps(s2, 0, CUTS[0])
                    dve.wait_ge(M["s_exp"], 9 * s2 + 9)
                    link(dve.tensor_tensor(st[0:n2, 82:90], st[0:n2, 58:66], st[0:n2, 74:82], ALU.add))
                    link(dve.reciprocal(st[0:n2, 82:90], st[0:n2, 82:90]))
                    dve.tensor_tensor(S[0:n2, :, c0:c1], S[0:n2, :, c0:c1], bc(st[0:n2, 82:90], c1 - c0, 2), ALU.mult).then_inc(M["p_ready"], 1)
                    conv_taps(s2, CUTS[0], CUTS[1])
                    pt = PTS if s2 == 0 else PT
                    kts = [1] if s2 == 1 else [0, 1]
                    seen = 0 if s2 == 0 else 2 * s2 - (1 if s2 >= 2 else 0)
                if 0 <= s3:
                    dve.wait_ge(M["ln2_done"], s3 + 1)
                    dve.tensor_copy(st[0:n3, 90:91], B[7][0:n3, 128:129]).then_inc(M["lnr_ready"], 1)
                if 0 <= s2 < NT:
                    conv_taps(s2, CUTS[1], CUTS[2])
                if 0 <= s3:
                    dve.wait_ge(M["ln_rs"], s3 + 1)
                    dve.tensor_scalar(LND[0:n3, 0:n3], ident[0:n3, 0:n3], st[0:n3, 91:92], float(CONV), ALU.mult, ALU.mult).then_inc(M["ln_diag"], 1)
                if 0 <= s2 < NT:
                    conv_taps(s2, CUTS[2], CUTS[3])
                if 0 <= s3:
                    dve.wait_ge(M["ln3_done"], s3 + 1)
                    link(dve.tensor_tensor(Y[s3], Y[s3], bc(B[7][:, 256:256 + n3], CC, 1), ALU.mult))
                    for c in range(CC):
                        dve.tensor_scalar(Y[s3][:, c, :], Y[s3][:, c, :], cvec[:, V_LNG + c:V_LNG + c + 1],
                                          cvec[:, V_LNB + c:V_LNB + c + 1], ALU.mult, ALU.add).then_inc(M["v_act"], 1)
                if 0 <= s2 < NT:
                    conv_taps(s2, CUTS[3], CUTS[4])
                if 0 <= s3:
                    tmp = TMP[:, 0:CC * n3]
                    dve.wait_ge(M["ln_exp"], s3 + 1)
                    link(dve.tensor_scalar(tmp, tmp, 1.0, None, ALU.add))
                    link(dve.reciprocal(tmp, tmp))
                    if s3 >= 1:
                        dve.wait_ge(M["wo_done"], 2 * s3)
                    dve.wait_ge(M["v_act"], CC * (s3 + 1))
                    dve.tensor_tensor(CT[:, :, 0:n3], Y[s3], tmp.rearrange("p (c t) -> p c t", c=CC), ALU.mult).then_inc(M["ct_ready"], 1)
                if 0 <= s2 < NT:
                    for k, kt in enumerate(kts):
                        nk = n2 if s2 == 0 and kt else 128
                        dve.wait_ge(M["ptD_done"], seen + k + 1)
                        dve.tensor_copy(pt[0:nk, kt, 4:8, :], B[1][0:nk, :].rearrange("p (h t) -> p h t", h=4)[:, :, 0:n2]).then_inc(M["ptD_ready"], 1)
                if s1 < NT:
                    dve.wait_ge(M["ub_exp"], s1 + 1)
                    link(dve.tensor_scalar(U[0:n1, :], U[0:n1, :], 1.0, None, ALU.add))
                    link(dve.reciprocal(U[0:n1, :], U[0:n1, :]))
                    dve.wait_ge(M["pua_done"], AFTER["pua_done"] + s1 + 1)
                    dve.tensor_tensor(U[0:n1, :], B[5][0:n1, :], U[0:n1, :], ALU.mult).then_inc(M["u_ready"], 1)
                    dve.wait_ge(M["qk_sq"], AFTER["qk_sq"] + 2 * s1 + 2)
                    if s1:
                        dve.wait_ge(M["qk_rs"], AFTER["qk_rs"] + s1)
                    if s1 >= 3:
                        dve.wait_ge(M["pvD_done"], s1 - 1)
                    dve.tensor_copy(VV[s1 % 3][0:n1, :], B[3][0:n1, 128:256]).then_inc(M["v_ready"], 1)
                    dve.tensor_reduce(st[0:n1, 12:20], Z[0:n1, 0:512].rearrange("p (h d) -> p h d", h=HEADS), X, ALU.add).then_inc(M["qk_ssq"], 1)
                    dve.tensor_reduce(st[0:n1, 20:22], KN[0:n1, :].rearrange("p (h d) -> p h d", h=KVH), X, ALU.add).then_inc(M["qk_ssq"], 1)
                    dve.wait_ge(M["qk_ssq"], AFTER["qk_ssq"] + 2 * s1 + 2)
                    if s1 + 1 < NT:
                        norm_z(s1 + 3, rows_of(s1 + 1), XR[(s1 + 3) % 4])
                    dve.wait_ge(M["qk_rs"], AFTER["qk_rs"] + s1 + 1)
                    qdst = QN[0:n1, :].rearrange("p (j k d) -> p k j d", j=4, k=2)
                    if s1:
                        dve.wait_ge(M["qT_done"], s1)
                    for kv in range(2):
                        a = dve.tensor_tensor(qdst[:, kv], B[2][0:n1, 256 * kv:256 * kv + 256].rearrange("p (j d) -> p j d", j=4),
                                              bc(st[0:n1, 22 + 4 * kv:26 + 4 * kv], HD, 2), ALU.mult)
                    a.then_inc(M["qn_ready"], 1)
                    kdst = KN[0:n1, :].rearrange("p (h d) -> p h d", h=KVH)
                    link(dve.tensor_tensor(kdst, B[3][0:n1, 0:128].rearrange("p (h d) -> p h d", h=KVH), bc(st[0:n1, 30:32], HD, 2), ALU.mult))
                    dve.tensor_tensor(kdst, kdst, bc(gk_bc[0:n1, :], KVH, 1), ALU.mult).then_inc(M["kn_ready"], 1)
                if 0 <= s2 < NT:
                    conv_taps(s2, CUTS[4], CC * TAPS)
                    if s2 + 1 < NT:
                        dve.wait_ge(M["conv_tap"], CC * TAPS * (s2 + 1))
                        if s2 == 0:
                            dve.memset(UT[1][:, :, 0:PAST], 0.0).then_inc(M["halo"], 1)
                        else:
                            dve.tensor_copy(UT[(s2 + 1) % 2][:, :, 0:PAST], UT[s2 % 2][:, :, 128:128 + PAST]).then_inc(M["halo"], 1)
                if 0 <= s3:
                    xr = XR[(s3 + 2) % 4]
                    for half in range(2):
                        dve.wait_ge(M["wo_done"], 2 * s3 + half + 1)
                        cols = slice(512 * half, 512 * half + 512)
                        dve.tensor_tensor(xr[0:n3, cols], B[half][0:n3, :], xr[0:n3, cols], ALU.add).then_inc(M["x1_ready"], 1)
                if 0 <= s2 < NT:
                    dve.wait_ge(M["pvD_done"], s2 + 1)
                    if s2 >= 1:
                        dve.wait_ge(M["wo_done"], 2 * s2)
                    dve.tensor_copy(OT[64:128, :, 0:n2], B[7][64:128, 0:4 * n2].rearrange("p (j t) -> p j t", j=4)).then_inc(M["otD_ready"], 1)

            norm_z(NT + 2, rows_of(0), XR[0])
            for it in range(NT + 2):
                s1, s2, s3 = it, it - 1, it - 2
                if s1 < NT:
                    n1 = rows_of(s1)
                    dve.wait_ge(M["mq_done"], AFTER["mq_done"] + 2 * s1) if s1 else dve.wait_ge(M["pua_done"], AFTER["pua_done"] + NT)
                    take_hT(s1 + NT + 2, n1, V_XA)
                if 0 <= s2 < NT:
                    n2 = rows_of(s2)
                    for half in range(2):
                        dve.wait_ge(M["q2T_done"], AFTER["q2T_done"] + 2 * s2 + half + 1)
                        g = cvec[:, V_MQ:V_MQ + 2][:, :, None].to_broadcast([128, 2, n2])
                        for r in range(2):
                            c = 4 * half + 2 * r
                            a = dve.tensor_tensor(QT2[:, c:c + 2, 0:n2], B[6 + half][:, 256 * r:256 * r + 256].rearrange("p (c t) -> p c t", c=2)[:, :, 0:n2], g, ALU.mult)
                        a.then_inc(M["q2T_ready"], 1)
                    if s2 == 0:
                        dve.wait_ge(M["qp2_zero"], AFTER["qp2_zero"] + 1)
                        dve.wait_ge(M["q2T_ready"], AFTER["q2T_ready"] + 2)
                        for b in range(DEC_B):
                            cols = slice(b * DEC_T, (b + 1) * DEC_T)
                            dve.tensor_copy(QP2[:, b, :, cols], QT2[:, :, cols]).then_inc(M["qp2_ready"], 1)
                        for b in range(DEC_B):
                            for mt in range(2):
                                dve.wait_ge(M["mkb_tD"], AFTER["mkb_tD"] + 2 * b + mt + 1)
                                if b:
                                    dve.wait_ge(M["mkb_used"], b)
                                dve.tensor_copy(MKTB[:, 4:8, mt * 128:(mt + 1) * 128], B[5][:, :].rearrange("p (c t) -> p c t", c=4)).then_inc(M["mkbD_ready"], 1)
                if 0 <= s3:
                    n3 = rows_of(s3)
                    dve.wait_ge(M["z3_rs"], s3 + 1)
                    if s3:
                        dve.wait_ge(M["z3_out"], 16 * s3)
                        dve.wait_ge(M["z3t_done"], 2 * s3)
                    dve.tensor_scalar(Z3[0:n3, :], XR[s3 % 4][0:n3, :], st[0:n3, 41:42], None, ALU.mult).then_inc(M["z3_ready"], 1)
                if 0 <= s2 < NT:
                    if s2 == 0:
                        dve.wait_ge(M["mkb_used"], DEC_B)
                    for half in range(2):
                        if s2:
                            dve.wait_ge(M["sc2_done"], AFTER["sc2_done"] + 2 * (s2 - 1) + half + 1)
                        a = dve.tensor_reduce(st[0:n2, 42 + 2 * half:44 + 2 * half], B[2 + half][0:n2, :].rearrange("p (h m) -> p h m", h=2), X, ALU.max)
                        a.then_inc(M["dve"], 1)
                        steps[0] += 1
                    dve.wait_ge(M["dve"], steps[0])
                    dve.tensor_scalar(st[0:n2, 50:54], st[0:n2, 42:46], -MSCALE, None, ALU.mult).then_inc(M["nm2_ready"], 1)
                    dve.wait_ge(M["s2_exp"], AFTER["s2_exp"] + 4 * s2 + 4)
                    link(dve.reciprocal(st[0:n2, 82:86], st[0:n2, 58:62]))
                    dve.tensor_tensor(S2[0:n2, :, :], S2[0:n2, :, :], bc(st[0:n2, 82:86], MEM, 2), ALU.mult).then_inc(M["p2_ready"], 1)
                    dve.wait_ge(M["pt2D_done"], AFTER["pt2D_done"] + s2 + 1)
                    if s2 == 1:
                        dve.wait_ge(M["mvb_used"], DEC_B)
                    if s2 >= 2:
                        dve.wait_ge(M["pv2D_done"], AFTER["pv2D_done"] + s2 - 1)
                    dve.tensor_copy(PT2[:, 1, :, 0:n2], B[1][:, :].rearrange("p (h t) -> p h t", h=4)[:, :, 0:n2]).then_inc(M["pt2D_ready"], 1)
                    if s2 == 0:
                        dve.wait_ge(M["mvb_used"], DEC_B)
                    else:
                        dve.wait_ge(M["pv2D_done"], AFTER["pv2D_done"] + s2)
                        dve.wait_ge(M["mo_done"], AFTER["mo_done"] + 2 * s2)
                    dve.tensor_copy(OT2[:, 4:8, 0:n2], B[7][:, :].rearrange("p (c t) -> p c t", c=4)[:, :, 0:n2]).then_inc(M["ot2D_ready"], 1)
                if 0 <= s3:
                    for half in range(2):
                        dve.wait_ge(M["z3t_done"], 2 * s3 + half + 1)
                        if s3:
                            dve.wait_ge(M["rt_done"], s3)
                        src = B[half][:, :].rearrange("p (c t) -> p c t", c=4)[:, :, 0:n3]
                        dve.tensor_tensor(H3[:, 4 * half:4 * half + 4, 0:n3], src, gain(V_FFN + 4 * half, 4, n3), ALU.mult).then_inc(M["h3_ready"], 1)
                    dve.wait_ge(M["rt_done"], s3 + 1)
                    if s3 == 0:
                        dve.wait_ge(M["moved_out"], 64)
                    dve.tensor_tensor(LG[0:n3, 36 * s3:36 * s3 + 36], B[2][0:n3, 0:36], br_bc[0:n3, :], ALU.add).then_inc(M["lg_ready"], 1)
                if s1 < NT:
                    dve.wait_ge(M["q2_sq"], AFTER["q2_sq"] + 2 * s1 + 2)
                    if s1:
                        dve.wait_ge(M["q2_rs"], AFTER["q2_rs"] + s1)
                    dve.tensor_reduce(st[0:n1, 32:36], Z[0:n1, :].rearrange("p (h d) -> p h d", h=MH), X, ALU.add).then_inc(M["q2_ssq"], 1)
                    dve.wait_ge(M["q2_ssq"], AFTER["q2_ssq"] + s1 + 1)
                    if s1 + 1 < NT:
                        norm_z(s1 + NT + 3, rows_of(s1 + 1), XR[(s1 + 1) % 4])
                    dve.wait_ge(M["q2_rs"], AFTER["q2_rs"] + s1 + 1)
                    if s1:
                        dve.wait_ge(M["q2T_done"], AFTER["q2T_done"] + 2 * s1)
                    for half in range(2):
                        dve.tensor_tensor(QN2[0:n1, 2 * half:2 * half + 2, :], B[4 + half][0:n1, :].rearrange("p (h d) -> p h d", h=2),
                                          bc(st[0:n1, 36 + 2 * half:38 + 2 * half], MHD, 2), ALU.mult).then_inc(M["q2n_ready"], 1)
                if 0 <= s2 < NT:
                    xr = XR[s2 % 4]
                    for k, half in enumerate((1, 0)):
                        dve.wait_ge(M["mo_done"], AFTER["mo_done"] + 2 * s2 + k + 1)
                        cols = slice(512 * half, 512 * half + 512)
                        dve.tensor_tensor(xr[0:n2, cols], B[2 + half][0:n2, :], xr[0:n2, cols], ALU.add).then_inc(M["x2_ready"], 1)

            dve.wait_ge(M["rconst_in"], 16)
            dve.wait_ge(M["lg_ready"], NT)
            lg = view(LG, 0, NT, 36)
            lgG, lgE = lg[:, :, 0:NG], lg[:, :, NG:36].rearrange("p t (g k) -> p t g k", g=NG)

            def first_max(oh, key, x, top, n):
                link(dve.tensor_reduce(top, x, X, ALU.max))
                link(dve.tensor_tensor(key, x, bc(top, n, 2), ALU.is_equal))
                link(dve.tensor_tensor(key, key, bc(down8[:, 8 - n:8], NT, 1), ALU.mult))
                link(dve.tensor_reduce(RT9, key, X, ALU.max))
                link(dve.tensor_tensor(oh, key, bc(RT9, n, 2), ALU.is_equal))

            link(dve.tensor_scalar(down8, iota[:, 0:8], -1.0, 8.0, ALU.mult, ALU.add))
            first_max(R_OG, R_K4, lgG, R_M1, NG)
            dve.tensor_tensor(R_EG, lgG, bc(R_M1, NG, 2), ALU.subtract).then_inc(M["r_arg"], 1)
            dve.wait_ge(M["r_exp"], 1)
            link(dve.tensor_reduce(R_PG, R_EG, X, ALU.add))
            link(dve.reciprocal(R_PG, R_PG))
            for g in range(NG):
                src = bc(R_OG[:, :, g], EPG, 2)
                if g == 0:
                    link(dve.tensor_tensor(R_SEL, lgE[:, :, g, :], src, ALU.mult))
                else:
                    link(dve.tensor_tensor(R_T8, lgE[:, :, g, :], src, ALU.mult))
                    link(dve.tensor_tensor(R_SEL, R_SEL, R_T8, ALU.add))
            first_max(R_O1, R_K8, R_SEL, R_M1, EPG)
            link(dve.scalar_tensor_tensor(R_SEL, R_O1, -3e38, R_SEL, ALU.mult, ALU.add))
            first_max(R_O2, R_K8, R_SEL, R_M2, EPG)
            dve.tensor_tensor(R_E2, R_M2, R_M1, ALU.subtract).then_inc(M["r_arg"], 1)
            dve.wait_ge(M["r_exp"], 2)
            link(dve.tensor_scalar(R_T9, R_E2, 1.0, None, ALU.add))
            link(dve.reciprocal(R_T9, R_T9))
            link(dve.tensor_tensor(gates[:, 0:NT], R_T9, R_PG, ALU.mult))
            link(dve.tensor_tensor(gates[:, NT:2 * NT], gates[:, 0:NT], R_E2, ALU.mult))
            for k, oh in enumerate((R_O1, R_O2)):
                for g in range(NG):
                    dst = RO[:, k * NT:(k + 1) * NT, g * EPG:(g + 1) * EPG]
                    link(dve.tensor_tensor(dst, oh, bc(R_OG[:, :, g], EPG, 2), ALU.mult))
            for k in range(2):
                link(dve.memset(RO[64:128, k * NT, :], 0.0))
            link(dve.tensor_tensor(RM3, RO[:, 0:NT, :], RO[:, NT:2 * NT, :], ALU.add))
            link(dve.memset(RA3[:, 0, :], 0.0))
            for s in range(1, NT):
                link(dve.tensor_tensor(RA3[:, s, :], RA3[:, s - 1, :], RM3[:, s - 1, :], ALU.add))
            dve.tensor_tensor(RTOT, RA3[:, NT - 1, :], RM3[:, NT - 1, :], ALU.add).then_inc(M["r_mask"], 1)
            dve.wait_ge(M["r_pref"], 1)
            link(dve.tensor_copy(R_CNT[0:32, :], B[1][0:32, 0:1]))
            link(dve.tensor_scalar(R_GT[0:32, :], thr[0:32, :], R_CNT[0:32, :], None, ALU.is_lt))
            link(dve.tensor_reduce(R_CNT[0:32, :], R_GT[0:32, :], X, ALU.add))
            dve.tensor_copy(ROV[0:32, :], R_CNT[0:32, 0:1].to_broadcast([32, 128])).then_inc(M["r_ov"], 1)
            for k in range(2):
                link(dve.tensor_tensor(RP3[:, k * NT:(k + 1) * NT, :], RO[:, k * NT:(k + 1) * NT, :],
                                       B[0][:, 0:288].rearrange("p (t e) -> p t e", t=NT), ALU.mult))
            link(dve.tensor_reduce(R_RANK, RP3, X, ALU.add))
            link(dve.tensor_tensor(RP3, RO, bc(iota[:, 0:NE], 2 * NT, 1), ALU.mult))
            link(dve.tensor_reduce(R_EXP, RP3, X, ALU.add))
            dve.wait_ge(M["r_base"], AFTER["r_base"] + 1)
            link(dve.tensor_copy(RBASE, B[1][:, 64:97]))
            link(dve.tensor_tensor(RP3, RO, bc(RBASE[:, 0:NE], 2 * NT, 1), ALU.mult))
            link(dve.tensor_reduce(R_BASE, RP3, X, ALU.add))
            link(dve.tensor_tensor(RG8, bc(R_RANK, 8, 2), bc(thr, 2 * NT, 1), ALU.is_ge))
            link(dve.tensor_reduce(R_FL, RG8, X, ALU.add))
            link(dve.scalar_tensor_tensor(R_ROW, R_FL, -128.0, R_RANK, ALU.mult, ALU.add))
            link(dve.tensor_tensor(R_BASE, R_BASE, R_FL, ALU.add))
            link(dve.tensor_scalar(R_BASE, R_BASE, float(NE - 1), None, ALU.add))
            link(dve.tensor_tensor(R_BASE, R_BASE, R_EXP, ALU.subtract))
            link(dve.tensor_scalar(R_FL, R_FL, 1.0, None, ALU.min))
            link(dve.tensor_tensor(R_BASE, R_BASE, R_FL, ALU.mult))
            link(dve.tensor_tensor(R_EXP, R_EXP, R_BASE, ALU.add))
            link(dve.scalar_tensor_tensor(R_RANK, R_EXP, 128.0, R_ROW, ALU.mult, ALU.add))
            link(dve.tensor_copy(slot_i[:, :], R_RANK))
            for k in range(2 * NT):
                dve.tensor_scalar(RR[:, k, :], iota, R_ROW[:, k:k + 1], None, ALU.is_equal)
                a = dve.tensor_scalar(RQ[:, k, :], iota[:, 0:NSLOT], R_EXP[:, k:k + 1], tok[:, k % NT:k % NT + 1], ALU.is_equal, ALU.mult)
            a.then_inc(M["r_rows"], 1)
            link(dve.tensor_tensor(RE3, bc(o16, NE, 2), bc(RBASE[:, 1:33], OVER, 1), ALU.is_ge))
            link(dve.tensor_reduce(R_EID, RE3, X, ALU.add))
            link(dve.tensor_scalar(R_EID, R_EID, float(NE - 1), None, ALU.min))
            link(dve.tensor_copy(eid_i[:, 0:OVER], R_EID))
            link(dve.tensor_copy(eid_i[:, OVER:OVER + 1], RBASE[:, 32:33]))
            dve.wait_ge(M["r_table"], AFTER["r_table"] + 1)
            dve.tensor_copy(idx_i[:, :], B[2][:, 0:NSLOT]).then_inc(M["route_ready"], 1)

            def take_rows(banks, buf, done, count, ready):
                for half in range(2):
                    dve.wait_ge(done, count + half)
                    dve.tensor_tensor(buf[:, 4 * half:4 * half + 4, :], B[half][:, :].rearrange("p (c t) -> p c t", c=4), gain(V_FFN + 4 * half, 4), ALU.mult).then_inc(ready, 1)

            def activate(p, e, a, sems, base):
                dve.tensor_scalar(e, e, 1.0, None, ALU.add).then_inc(sems, 1)
                dve.wait_ge(sems, base + 1)
                dve.reciprocal(e, e).then_inc(sems, 1)
                dve.wait_ge(sems, base + 2)
                dve.tensor_tensor(e, B[2 + p][:, 0:FE], e, ALU.mult).then_inc(sems, 1)
                dve.wait_ge(sems, base + 3)
                return dve.tensor_tensor(a, B[2 + p][:, FE:2 * FE], e, ALU.mult)

            def expert_step(n, u, first, more1, more2):
                p = u % 2
                dve.wait_ge(M["gu_exp"], n + 1)
                if not first:
                    dve.wait_ge(M["at_done"], n - 1)
                activate(p, EB[p], AB[p], M["ex_chain"], n * 3).then_inc(M["ab_ready"], 1)
                if more2:
                    take_rows(None, HG[p], M["zt4_done"], n * 2 + 5, M["hg_ready"])
                if not first:
                    dve.wait_ge(y_out[p], (n // 2) * 16 if isinstance(n, int) else (n - u) * 8 + (u // 2) * 16)
                dve.wait_ge(M["dn_done"], n * 2 + 2)
                dve.tensor_copy(YB[p][:, 512:1024], B[7][:, :]).then_inc(M["yb_readyD"], 1)

            take_rows(None, HG[0], M["zt4_done"], 1, M["hg_ready"])
            take_rows(None, HG[1], M["zt4_done"], 3, M["hg_ready"])
            for u in range(4):
                expert_step(u, u, u < 2, True, True)
            with dve.Fori(1, NE // 4 - 1) as it:
                for u in range(4):
                    expert_step(it * 4 + u, u, False, True, True)
            for u in range(4):
                n = NE - 4 + u
                expert_step(n, u, False, n + 1 < NE, n + 2 < NE)
            dve.wait_ge(y_out[0], 16 * NE // 2)
            total = dve.value_load(eid_i[0:1, OVER:OVER + 1], min_val=0, max_val=OVER)
            with dve.Fori(0, OVER) as n:
                with dve.If(total > n):
                    take_rows(None, HG[0], M["over_t"], n * 2 + (2 * NE + 1), M["over_h"])
                    dve.wait_ge(M["over_e"], AFTER["over_e"] + n + 1)
                    activate(0, EB[0], AB[0], M["ex_chain"], n * 3 + 3 * NE).then_inc(M["ab_ready"], 1)
                    dve.wait_ge(y_out[0], n * 16 + 8 * NE)
                    dve.wait_ge(M["over_dn"], AFTER["over_dn"] + n * 2 + 2)
                    dve.tensor_copy(YB[0][:, 512:1024], B[7][:, :]).then_inc(M["over_yD"], 1)
            for s in range(NT):
                n = rows_of(s)
                k = s % 2
                dve.wait_ge(cx_in[k], 16 * (s // 2 + 1))
                dve.wait_ge(cy_in[2 * k], 16 * (s // 2 + 1))
                if s >= 2:
                    dve.wait_ge(co_out[k], 16 * (s // 2))
                dve.scalar_tensor_tensor(CO[k][0:n, :], CY[2 * k][0:n, :], gates[0:n, s:s + 1], CX[k][0:n, :], ALU.mult, ALU.add).then_inc(M["co_done"], 1)
                dve.wait_ge(M["co_done"], s + 1)
                dve.wait_ge(cy_in[2 * k + 1], 16 * (s // 2 + 1))
                dve.scalar_tensor_tensor(CO[k][0:n, :], CY[2 * k + 1][0:n, :], gates[0:n, NT + s:NT + s + 1], CO[k][0:n, :], ALU.mult, ALU.add).then_inc(M["co_ready"], 1)


_INS = ["x_prompt", "x_sample", "cache_swa_k", "cache_swa_v", "state_conv", "cache_mem_k", "cache_mem_v", "mem_prompt",
        "norm_mix_g", "w_in", "q_norm_g", "k_norm_g", "attn_sinks", "conv_dw_w", "conv_dw_b", "conv_ln_g", "conv_ln_b", "w_out",
        "norm_xa_g", "norm_mem_g", "w_mq", "w_mk", "w_mv", "mq_norm_g", "mk_norm_g", "w_mo",
        "norm_ffn_g", "w_router_group", "b_router_group", "w_router_expert", "b_router_expert",
        "w_exp_gate", "w_exp_up", "w_exp_down"]
_OUTS = [("y_p", (1, SEQ, D)), ("y_s", (DEC_B, DEC_T, D)), ("swa_k_p", (1, 1, 128, KVH, HD)), ("swa_v_p", (1, 1, 128, KVH, HD)),
         ("conv_p", (1, 1, PAST, CONV)), ("mem_k", (1, 1, MEM, MH, MHD)), ("mem_v", (1, 1, MEM, MH, MHD)),
         ("swa_k_s", (1, DEC_B, 128, KVH, HD)), ("swa_v_s", (1, DEC_B, 128, KVH, HD)), ("conv_s", (1, DEC_B, PAST, CONV))]


def kernel(**inputs):
    import concourse.bacc as _bacc
    from concourse.bass_utils import run_bass_kernel_spmd as _run

    nc = _bacc.Bacc("TRN2", target_bir_lowering=False, num_devices=1)
    f32 = mybir.dt.float32
    arrays, i, o = {}, {}, {}
    for name in _INS:
        a = np.ascontiguousarray(inputs[name])
        arrays["in_" + name] = a
        i[name] = nc.dram_tensor("in_" + name, a.shape, f32, kind="ExternalInput").ap()
    arrays["in_consts"] = shape_constants()
    i["consts"] = nc.dram_tensor("in_consts", (128, NCONST), f32, kind="ExternalInput").ap()
    for name, shape in _OUTS:
        o[name] = nc.dram_tensor("out_" + name, shape, f32, kind="ExternalOutput").ap()
    build(nc, i, o)
    r = _run(nc, [arrays], core_ids=[0])
    return tuple(r.results[0]["out_" + name] for name, _ in _OUTS)
```
